# Optimizing a Trainium2 kernel written in Bass

```python
import math
import jax
import jax.numpy as jnp
from jax import lax
import numpy as np

D_MODEL = 2048
BATCH = 1
SEQ = 256
DEPTH = 1
DEC_BATCH = 8
DEC_SEQ = 16
PAST_LEN = 512

CHUNK = 64
CONV_WIDTH = 4
RMS_EPS = 1e-6
SSM_INNER = D_MODEL
SSM_HEAD_DIM = 64
SSM_HEADS = SSM_INNER // SSM_HEAD_DIM
SSM_GROUPS = 4
SSM_HEADS_PER_GROUP = SSM_HEADS // SSM_GROUPS
SSM_STATE = 128
SSM_CONV_DIM = SSM_INNER + 2 * SSM_GROUPS * SSM_STATE
LRU_WIDTH = D_MODEL
LRU_BLOCKS = 16
LRU_BLOCK_WIDTH = LRU_WIDTH // LRU_BLOCKS
LRU_C = 8.0
N_EXPERT_GROUPS = 4
EXPERTS_PER_GROUP = 8
N_EXPERTS = N_EXPERT_GROUPS * EXPERTS_PER_GROUP
TOP_K = 2
EXPERT_FF = D_MODEL // 4
MOE_BLOCK = 256
PLE_DIM = 256
OFF_Z = SSM_INNER
OFF_XBC = OFF_Z + SSM_CONV_DIM
OFF_DT = OFF_XBC + SSM_HEADS
OFF_GY = OFF_DT + LRU_WIDTH
OFF_XL = OFF_GY + LRU_WIDTH
OFF_GM = OFF_XL + D_MODEL
IN_DIM = OFF_GM + D_MODEL

kernel_name = 'hybrid_ssd_rglru_hiermoe_stream_step'

def _rms_norm(x, g):
    x32 = x.astype(jnp.float32)
    y = x32 * lax.rsqrt(jnp.mean(x32 * x32, axis=-1, keepdims=True) + RMS_EPS)
    return (y * g.astype(jnp.float32)).astype(x.dtype)

def _causal_conv(x, buf, w, bias):
    xp = jnp.concatenate([buf.astype(x.dtype), x], axis=1)
    y = lax.conv_general_dilated(xp, w[:, None, :].astype(x.dtype), window_strides=(1,), padding='VALID',
                                 dimension_numbers=('NWC', 'WIO', 'NWC'), feature_group_count=x.shape[-1])
    return y + bias.astype(x.dtype), xp[:, -(CONV_WIDTH - 1):]

def _ssd(x, dt, a_neg, bm, cm, h0):
    f32 = jnp.float32
    b, L = x.shape[:2]
    G, HG, P, N = SSM_GROUPS, SSM_HEADS_PER_GROUP, SSM_HEAD_DIM, SSM_STATE
    pad = (-L) % CHUNK
    c = (L + pad) // CHUNK

    def chunked(t):
        t = jnp.pad(t.astype(f32), [(0, 0), (0, pad)] + [(0, 0)] * (t.ndim - 2))
        return t.reshape((b, c, CHUNK) + t.shape[2:])

    xc = chunked(x).reshape(b, c, CHUNK, G, HG, P)
    dtc = chunked(dt).reshape(b, c, CHUNK, G, HG)
    bc = chunked(bm)
    cc = chunked(cm)
    a_cum = jnp.cumsum(dtc * a_neg.astype(f32).reshape(G, HG), axis=2)
    causal = jnp.tril(jnp.ones((CHUNK, CHUNK), dtype=bool))[None, None, :, :, None, None]
    seg = a_cum[:, :, :, None] - a_cum[:, :, None, :]
    decay_in = jnp.exp(jnp.where(causal, seg, -jnp.inf))
    xdt = xc * dtc[..., None]
    cb = jnp.einsum('bclgn,bcsgn->bclsg', cc, bc)
    y_diag = jnp.einsum('bclsg,bclsgh,bcsghp->bclghp', cb, decay_in, xdt)
    decay_out = jnp.exp(a_cum[:, :, -1:] - a_cum)
    chunk_states = jnp.einsum('bcsgn,bcsgh,bcsghp->bcghpn', bc, decay_out, xdt)
    chunk_decay = jnp.exp(a_cum[:, :, -1])

    def step(h, inp):
        dec, st = inp
        return dec[..., None, None] * h + st, h

    h_last, h_prev = lax.scan(step, h0.astype(f32).reshape(b, G, HG, P, N),
                              (jnp.moveaxis(chunk_decay, 1, 0), jnp.moveaxis(chunk_states, 1, 0)))
    h_prev = jnp.moveaxis(h_prev, 0, 1)
    y_off = jnp.einsum('bclgn,bcghpn,bclgh->bclghp', cc, h_prev, jnp.exp(a_cum))
    y = (y_diag + y_off).reshape(b, c * CHUNK, SSM_HEADS, P)[:, :L]
    return y, h_last.reshape(b, SSM_HEADS, P, N)

def _rg_lru(x, h0, w_a, b_a, w_x, b_x, lam):
    f32 = jnp.float32
    b, L, _ = x.shape
    x32 = x.astype(f32)
    xb = x32.reshape(b, L, LRU_BLOCKS, LRU_BLOCK_WIDTH)
    r = jax.nn.sigmoid(jnp.einsum('blnk,nkj->blnj', xb, w_a.astype(f32)).reshape(b, L, LRU_WIDTH) + b_a.astype(f32))
    i = jax.nn.sigmoid(jnp.einsum('blnk,nkj->blnj', xb, w_x.astype(f32)).reshape(b, L, LRU_WIDTH) + b_x.astype(f32))
    log_a = -LRU_C * r * jax.nn.softplus(-lam.astype(f32))
    a = jnp.exp(log_a)
    u = jnp.sqrt(-jnp.expm1(2.0 * log_a)) * (i * x32)
    u = u.at[:, 0].add(a[:, 0] * h0.astype(f32))

    def combine(left, right):
        a_l, u_l = left
        a_r, u_r = right
        return a_l * a_r, a_r * u_l + u_r

    _, h = lax.associative_scan(combine, (a, u), axis=1)
    return h, h[:, -1]

def _hier_moe(x2, w_rg, b_rg, w_re, b_re, w_gate, w_up, w_down):
    f32 = jnp.float32
    T = x2.shape[0]
    x32 = x2.astype(f32)
    g_prob = jax.nn.softmax(x32 @ w_rg.astype(f32) + b_rg.astype(f32), axis=-1)
    g_w, g_idx = lax.top_k(g_prob, 1)
    e_logit = (x32 @ w_re.astype(f32) + b_re.astype(f32)).reshape(T, N_EXPERT_GROUPS, EXPERTS_PER_GROUP)
    e_logit = jnp.take_along_axis(e_logit, g_idx[:, :, None], axis=1)[:, 0]
    e_w, e_local = lax.top_k(jax.nn.softmax(e_logit, axis=-1), TOP_K)
    e_w = e_w / jnp.sum(e_w, axis=-1, keepdims=True)
    weight = (g_w * e_w).reshape(-1)
    expert = (g_idx * EXPERTS_PER_GROUP + e_local).reshape(-1).astype(jnp.int32)
    n_assign = T * TOP_K
    blk = max(8, min(MOE_BLOCK, n_assign // N_EXPERTS))
    n_blocks = -(-n_assign // blk) + N_EXPERTS
    order = jnp.argsort(expert)
    sorted_e = expert[order]
    token = (order // TOP_K).astype(jnp.int32)
    counts = jnp.bincount(expert, length=N_EXPERTS)
    padded = (counts + blk - 1) // blk * blk
    pad_end = jnp.cumsum(padded)
    pad_start = pad_end - padded
    seg_start = jnp.cumsum(counts) - counts
    dest = pad_start[sorted_e] + jnp.arange(n_assign) - seg_start[sorted_e]
    row_token = jnp.zeros((n_blocks * blk,), jnp.int32).at[dest].set(token)
    block_expert = jnp.minimum(jnp.searchsorted(pad_end, jnp.arange(n_blocks) * blk, side='right'), N_EXPERTS - 1)

    def expert_block(args):
        rows, e = args
        xb = x2[rows]
        hdn = jax.nn.silu(xb @ w_gate[e]) * (xb @ w_up[e])
        return hdn @ w_down[e]

    ys = lax.map(expert_block, (row_token.reshape(n_blocks, blk), block_expert)).reshape(n_blocks * blk, -1)
    contrib = ys[dest] * weight[order][:, None].astype(ys.dtype)
    return jnp.zeros_like(x2).at[token].add(contrib)

def _layer(x, p, ssm0, sconv0, lru0, lconv0, lp):
    f32 = jnp.float32
    b, L, _ = x.shape
    xn = _rms_norm(x, lp['g_mix'])
    proj = xn @ lp['w_in']
    z, xbc, dt_raw, gate_y, x_lru, gate_m, gate_r = jnp.split(proj, [OFF_Z, OFF_XBC, OFF_DT, OFF_GY, OFF_XL, OFF_GM], axis=-1)
    xbc, sconv_new = _causal_conv(xbc, sconv0, lp['conv_m_w'], lp['conv_m_b'])
    xbc = jax.nn.silu(xbc)
    xs, bm, cm = jnp.split(xbc, [SSM_INNER, SSM_INNER + SSM_GROUPS * SSM_STATE], axis=-1)
    xs = xs.reshape(b, L, SSM_HEADS, SSM_HEAD_DIM)
    dt = jax.nn.softplus(dt_raw.astype(f32) + lp['dt_bias'].astype(f32))
    y_ssm, ssm_new = _ssd(xs, dt, -jnp.exp(lp['a_log'].astype(f32)),
                          bm.reshape(b, L, SSM_GROUPS, SSM_STATE), cm.reshape(b, L, SSM_GROUPS, SSM_STATE), ssm0)
    y_ssm = y_ssm + lp['d_skip'].astype(f32)[:, None] * xs.astype(f32)
    y_ssm = _rms_norm(y_ssm.reshape(b, L, SSM_INNER) * jax.nn.silu(z.astype(f32)), lp['g_ssm']).astype(x.dtype)
    o_m = y_ssm @ lp['w_out_m']
    xl, lconv_new = _causal_conv(x_lru, lconv0, lp['conv_r_w'], lp['conv_r_b'])
    h, lru_new = _rg_lru(xl, lru0, lp['w_lru_a'], lp['b_lru_a'], lp['w_lru_x'], lp['b_lru_x'], lp['lru_lambda'])
    o_r = (h.astype(x.dtype) * jax.nn.gelu(gate_y)) @ lp['w_out_r']
    mixed = jax.nn.sigmoid(gate_m) * o_m + jax.nn.sigmoid(gate_r) * o_r
    x = x + mixed @ lp['w_o']
    xn2 = _rms_norm(x, lp['g_ffn'])
    x = x + _hier_moe(xn2.reshape(b * L, D_MODEL), lp['w_router_group'], lp['b_router_group'],
                      lp['w_router_expert'], lp['b_router_expert'], lp['w_exp_gate'], lp['w_exp_up'],
                      lp['w_exp_down']).reshape(b, L, D_MODEL)
    ple_gate = jax.nn.sigmoid(_rms_norm(x, lp['g_ple']) @ lp['w_ple_gate'])
    x = x + ple_gate * (p.astype(x.dtype) @ lp['w_ple'])
    return x, ssm_new, sconv_new, lru_new, lconv_new

def setup_inputs(seed: int = 0) -> dict:
    key = jax.random.key(seed)
    ks = iter(jax.random.split(key, 64))

    def nrm(shape, scale):
        return jax.random.normal(next(ks), shape, jnp.float32) * scale

    def gain(shape):
        return 1.0 + nrm(shape, 0.02)

    dt0 = jnp.exp(jax.random.uniform(next(ks), (DEPTH, SSM_HEADS), jnp.float32, math.log(1e-3), math.log(1e-1)))
    a0 = jax.random.uniform(next(ks), (DEPTH, LRU_WIDTH), jnp.float32, 0.9, 0.999)
    return {
        'x_prompt': nrm((BATCH, SEQ, D_MODEL), 1.0),
        'x_sample': nrm((DEC_BATCH, DEC_SEQ, D_MODEL), 1.0),
        'state_ssm': nrm((DEPTH, DEC_BATCH, SSM_HEADS, SSM_HEAD_DIM, SSM_STATE), 0.5),
        'state_ssm_conv': nrm((DEPTH, DEC_BATCH, CONV_WIDTH - 1, SSM_CONV_DIM), 1.0),
        'state_lru': nrm((DEPTH, DEC_BATCH, LRU_WIDTH), 0.5),
        'state_lru_conv': nrm((DEPTH, DEC_BATCH, CONV_WIDTH - 1, LRU_WIDTH), 1.0),
        'p_prompt': nrm((DEPTH, BATCH, SEQ, PLE_DIM), 1.0),
        'p_sample': nrm((DEPTH, DEC_BATCH, DEC_SEQ, PLE_DIM), 1.0),
        'g_mix': gain((DEPTH, D_MODEL)),
        'w_in': nrm((DEPTH, D_MODEL, IN_DIM), D_MODEL ** -0.5),
        'conv_m_w': nrm((DEPTH, CONV_WIDTH, SSM_CONV_DIM), 0.5),
        'conv_m_b': nrm((DEPTH, SSM_CONV_DIM), 0.01),
        'dt_bias': dt0 + jnp.log(-jnp.expm1(-dt0)),
        'a_log': jnp.log(jax.random.uniform(next(ks), (DEPTH, SSM_HEADS), jnp.float32, 1.0, 16.0)),
        'd_skip': gain((DEPTH, SSM_HEADS)),
        'g_ssm': gain((DEPTH, SSM_INNER)),
        'w_out_m': nrm((DEPTH, SSM_INNER, D_MODEL), SSM_INNER ** -0.5),
        'conv_r_w': nrm((DEPTH, CONV_WIDTH, LRU_WIDTH), 0.5),
        'conv_r_b': nrm((DEPTH, LRU_WIDTH), 0.01),
        'w_lru_a': nrm((DEPTH, LRU_BLOCKS, LRU_BLOCK_WIDTH, LRU_BLOCK_WIDTH), LRU_BLOCK_WIDTH ** -0.5),
        'b_lru_a': nrm((DEPTH, LRU_WIDTH), 0.01),
        'w_lru_x': nrm((DEPTH, LRU_BLOCKS, LRU_BLOCK_WIDTH, LRU_BLOCK_WIDTH), LRU_BLOCK_WIDTH ** -0.5),
        'b_lru_x': nrm((DEPTH, LRU_WIDTH), 0.01),
        'lru_lambda': jnp.log(a0) - jnp.log1p(-a0),
        'w_out_r': nrm((DEPTH, LRU_WIDTH, D_MODEL), LRU_WIDTH ** -0.5),
        'w_o': nrm((DEPTH, D_MODEL, D_MODEL), D_MODEL ** -0.5),
        'g_ffn': gain((DEPTH, D_MODEL)),
        'w_router_group': nrm((DEPTH, D_MODEL, N_EXPERT_GROUPS), D_MODEL ** -0.5),
        'b_router_group': nrm((DEPTH, N_EXPERT_GROUPS), 0.01),
        'w_router_expert': nrm((DEPTH, D_MODEL, N_EXPERTS), D_MODEL ** -0.5),
        'b_router_expert': nrm((DEPTH, N_EXPERTS), 0.01),
        'w_exp_gate': nrm((DEPTH, N_EXPERTS, D_MODEL, EXPERT_FF), D_MODEL ** -0.5),
        'w_exp_up': nrm((DEPTH, N_EXPERTS, D_MODEL, EXPERT_FF), D_MODEL ** -0.5),
        'w_exp_down': nrm((DEPTH, N_EXPERTS, EXPERT_FF, D_MODEL), EXPERT_FF ** -0.5),
        'g_ple': gain((DEPTH, D_MODEL)),
        'w_ple_gate': nrm((DEPTH, D_MODEL, D_MODEL), D_MODEL ** -0.5),
        'w_ple': nrm((DEPTH, PLE_DIM, D_MODEL), PLE_DIM ** -0.5),
        'g_final': gain((D_MODEL,)),
    }

def reference(x_prompt, x_sample, state_ssm, state_ssm_conv, state_lru, state_lru_conv, p_prompt, p_sample,
              g_mix, w_in, conv_m_w, conv_m_b, dt_bias, a_log, d_skip, g_ssm, w_out_m,
              conv_r_w, conv_r_b, w_lru_a, b_lru_a, w_lru_x, b_lru_x, lru_lambda, w_out_r, w_o,
              g_ffn, w_router_group, b_router_group, w_router_expert, b_router_expert,
              w_exp_gate, w_exp_up, w_exp_down, g_ple, w_ple_gate, w_ple, g_final):
    bp = x_prompt.shape[0]
    hp = x_prompt
    hs = x_sample
    ssm_p, sconv_p, lru_p, lconv_p = [], [], [], []
    ssm_s, sconv_s, lru_s, lconv_s = [], [], [], []
    for i in range(DEPTH):
        lp = {
            'g_mix': g_mix[i], 'w_in': w_in[i], 'conv_m_w': conv_m_w[i], 'conv_m_b': conv_m_b[i],
            'dt_bias': dt_bias[i], 'a_log': a_log[i], 'd_skip': d_skip[i], 'g_ssm': g_ssm[i],
            'w_out_m': w_out_m[i], 'conv_r_w': conv_r_w[i], 'conv_r_b': conv_r_b[i],
            'w_lru_a': w_lru_a[i], 'b_lru_a': b_lru_a[i], 'w_lru_x': w_lru_x[i], 'b_lru_x': b_lru_x[i],
            'lru_lambda': lru_lambda[i], 'w_out_r': w_out_r[i], 'w_o': w_o[i], 'g_ffn': g_ffn[i],
            'w_router_group': w_router_group[i], 'b_router_group': b_router_group[i],
            'w_router_expert': w_router_expert[i], 'b_router_expert': b_router_expert[i],
            'w_exp_gate': w_exp_gate[i], 'w_exp_up': w_exp_up[i], 'w_exp_down': w_exp_down[i],
            'g_ple': g_ple[i], 'w_ple_gate': w_ple_gate[i], 'w_ple': w_ple[i],
        }
        zero_ssm = jnp.zeros((bp, SSM_HEADS, SSM_HEAD_DIM, SSM_STATE), jnp.float32)
        zero_sconv = jnp.zeros((bp, CONV_WIDTH - 1, SSM_CONV_DIM), x_prompt.dtype)
        zero_lru = jnp.zeros((bp, LRU_WIDTH), jnp.float32)
        zero_lconv = jnp.zeros((bp, CONV_WIDTH - 1, LRU_WIDTH), x_prompt.dtype)
        hp, a1, a2, a3, a4 = _layer(hp, p_prompt[i], zero_ssm, zero_sconv, zero_lru, zero_lconv, lp)
        ssm_p.append(a1)
        sconv_p.append(a2)
        lru_p.append(a3)
        lconv_p.append(a4)
        hs, b1, b2, b3, b4 = _layer(hs, p_sample[i], state_ssm[i], state_ssm_conv[i], state_lru[i], state_lru_conv[i], lp)
        ssm_s.append(b1)
        sconv_s.append(b2)
        lru_s.append(b3)
        lconv_s.append(b4)
    y_prompt = _rms_norm(hp, g_final)
    y_sample = _rms_norm(hs, g_final)
    return (y_prompt, y_sample,
            jnp.stack(ssm_p), jnp.stack(sconv_p), jnp.stack(lru_p), jnp.stack(lconv_p),
            jnp.stack(ssm_s), jnp.stack(sconv_s), jnp.stack(lru_s), jnp.stack(lconv_s))


_drawn_inputs = setup_inputs


def setup_inputs(seed=0):
    import zlib

    import numpy as np

    out = dict(_drawn_inputs(seed))
    spreads = {}
    factors = {'conv_m_b': 3.534,
     'd_skip': 11.897,
     'b_lru_a': 24.334,
     'b_lru_x': 8.0,
     'b_router_group': 35.755,
     'b_router_expert': 4.625,
     'g_ple': 42.863,
     'g_final': 8.101}
    for name, (base, spread) in spreads.items():
        noise = np.random.default_rng([zlib.crc32(name.encode()), seed]).standard_normal(out[name].shape)
        drawn = base * np.exp(spread * noise) if base else spread * noise
        out[name] = jnp.asarray(drawn.astype(out[name].dtype))
    for name, factor in factors.items():
        out[name] = (out[name] * factor).astype(out[name].dtype)
    return out
```

```python
import concourse.bass as bass
from concourse import mybir
from contextlib import ExitStack

PARAM_DMAS, CONSTS = 13, 14
SSD_LINKS, LRU_LINKS = 50, 24

D = 2048
KC = D // 128
SEQ, NSEQ, SLEN = 256, 8, 16
T = SEQ + NSEQ * SLEN
NT = T // 128
HEADS, HP, NST, GROUPS = 32, 64, 128, 4
HPG = HEADS // GROUPS
XBC = D + 2 * GROUPS * NST
TAPS = 4
HIST = TAPS - 1
PADDED = HIST + SEQ + NSEQ * (HIST + SLEN)
CONV = PADDED - HIST
S0 = SEQ + HIST
SPAD = SLEN + HIST
OFF_Z, OFF_X = 0, D
OFF_B, OFF_C = OFF_X + D, OFF_X + D + GROUPS * NST
OFF_DT = OFF_X + XBC
OFF_GY = OFF_DT + HEADS
OFF_XL = OFF_GY + D
OFF_GM = OFF_XL + D
OFF_GR = OFF_GM + D
EG, EPG = 4, 8
NE = EG * EPG
FF = D // 4
FC = FF // 128
SLOTS = 64
PASSES = T // SLOTS
PAIRS = NE // 2
PLE = 256
EPS = 1e-6
SLAB = 256
SLABF = KC * SLAB
BIG = 1.0e30

P_GMIX, P_GFFN, P_GPLE, P_GSSM = 0, 16, 32, 48
P_BA, P_BX, P_LAM, P_CB = 64, 80, 96, 112
P_CW = 152
P_CR = P_CW + TAPS * 24
P_ROWS = P_CR + TAPS * 16
NCONV = 40

C_DT, C_CUM, C_DD, C_DDF = 0, 3, 6, 9


def hybrid_stream_step(nc, a, outs, scr):
    fp32, i32, fp16 = mybir.dt.float32, mybir.dt.int32, mybir.dt.float16
    ALU, ACT, AX = mybir.AluOpType, mybir.ActivationFunctionType, mybir.AxisListType
    ds = bass.ds
    (y_p, y_s, ssm_p, sconv_p, lru_p, lconv_p, ssm_s, sconv_s, lru_s, lconv_s) = outs
    acum_d, xn_d, y_d = scr

    ctx = ExitStack()
    with ctx:
        arena = ctx.enter_context(nc.sbuf_tensor("arena", [128, 53200], fp32))
        banks = [ctx.enter_context(nc.psum_tensor(f"bank{i}", [128, 512], fp32)) for i in range(8)]

        def sem(name):
            return ctx.enter_context(nc.semaphore(name))

        class Region:
            def __init__(self, start, size):
                self.at, self.end = start, start + size

            def take(self, n, parts=128):
                self.at += n
                assert self.at <= self.end, (self.at, self.end)
                return arena[0:parts, self.at - n:self.at]

        def v3(ap, x):
            return ap.rearrange("p (x y) -> p x y", x=x)

        RING, RA, RY, RH, RT = 0, 6 * SLABF, 6 * SLABF + 6144, 6 * SLABF + 2 * 6144, 6 * SLABF + 3 * 6144
        slot = [arena[:, s * SLABF:(s + 1) * SLABF] for s in range(6)]
        slab = [v3(s, KC) for s in slot]
        xnT = v3(arena[:, RA:RA + 6144], KC)
        x_res = v3(arena[:, RA:RA + 6144], NT)
        Y = v3(arena[:, RY:RY + 6144], KC)
        H = v3(arena[:, RH:RH + 6144], KC)
        x_in = v3(arena[:, RH:RH + 6144], NT)
        hist_rows = arena[0:NSEQ * HIST, RY:RY + XBC + D]

        keep = Region(RT, 4040)
        ident = keep.take(128)
        ones = keep.take(128)
        before = keep.take(128)
        causal = v3(keep.take(256), 2)
        stream_of = keep.take(NSEQ)
        pcol = keep.take(384)
        convmem = v3(keep.take(NCONV * 27), NCONV)
        tokcol = v3(keep.take(10 * HEADS), 10)
        lru_h0 = v3(keep.take(128), NSEQ)
        lru_end = v3(keep.take(16 * 9), 9)
        ss_acc = keep.take(T)
        rstdB = keep.take(T)
        dskip = keep.take(KC)
        lam_c = keep.take(KC)
        sm = keep.take(256)
        iota64 = keep.take(64)
        rtail = Region(keep.at, RT + 10192 - keep.at)
        mixed = v3(rtail.take(6144), KC)
        under = Region(RT + keep.at - RT, 6144)
        raw = [under.take(PADDED) for _ in range(2)]
        acc = [under.take(PADDED) for _ in range(2)]

        rs = Region(3 * SLABF, 3 * SLABF)
        decay = v3(rs.take(HPG * T), HPG)
        growth = v3(rs.take(4 * T), 4)
        xsT = v3(rs.take(4 * T), 4)
        x_dt = v3(rs.take(NT * 512), NT)
        x_dd = v3(rs.take(NT * 512), NT)
        h0 = [v3(rs.take(NSEQ * NST), NSEQ) for _ in range(2)]
        x_ddf = rs.take(512)
        hT0 = rs.take(512)
        rh = Region(RH, 6144)
        h0T = v3(rh.take(NSEQ * 128), NSEQ)
        Bseg = v3(rh.take(NSEQ * NST), NSEQ)
        BT, CT = rh.take(T), rh.take(T)
        Btok = v3(rh.take(NT * NST), NT)
        cbm = v3(rh.take(NT * 128), NT)
        pst = v3(rh.take(512), 4)
        ytmp = [rh.take(T) for _ in range(2)]
        ysq = [rh.take(T) for _ in range(2)]
        dec = rh.take(NSEQ)

        rl = Region(3 * SLABF, 3 * SLABF)
        xl, gy, lr, li, la_, lt = (v3(rl.take(4 * T), 4) for _ in range(6))
        lw = v3(slot[2][:, 0:1024], 8)

        rm = Region(3 * SLABF, SLABF)
        sg_m, sg_r, t_m, t_r = ([rm.take(T) for _ in range(2)] for _ in range(4))

        rd = Region(3 * SLABF, SLABF)
        dtT, dA, cumT, ddT, dtmp, dtmp2, rmask = (rd.take(T, 32) for _ in range(7))
        ddfT = rd.take(128, 32)
        dcol = rd.take(8, 32)
        w_dt = v3(slot[2][:, 0:KC * HEADS], KC)
        nrm = [slot[4][:, 0:D], slot[4][:, D:2 * D]]
        prow = v3(slot[5][:, 0:384], 3)
        consts_ready = sem("consts_ready")
        params_in = sem("params_in")
        setup_in = sem("setup_in")
        x_loaded = sem("x_loaded")
        ptr_done = sem("ptr_done")
        hist_T, hist_evac = sem("hist_T"), sem("hist_evac")
        n_sq, n_ms, n_rt, n_scaled = sem("n_sq"), sem("n_ms"), sem("n_rt"), sem("n_scaled")
        n_tr, n_evac = sem("n_tr"), sem("n_evac")
        dt_loaded, dt_done, dt_step, dt_act = sem("dt_loaded"), sem("dt_done"), sem("dt_step"), sem("dt_act")
        dt_tr, cum_stored = sem("dt_tr"), sem("cum_stored")
        slab_loaded = [sem("slab_loaded0"), sem("slab_loaded1")]
        side_loaded = sem("side_loaded")
        proj_done, proj_free = sem("proj_done"), sem("proj_free")
        raw_ready, raw_free = sem("raw_ready"), sem("raw_free")
        conv_done, acc_free = sem("conv_done"), sem("acc_free")
        silu_done, z_done = sem("silu_done"), sem("z_done")
        cum_loaded, seg_ready, exp_done = sem("cum_loaded"), sem("seg_ready"), sem("exp_done")
        aux_done, aux_evac, w_ready = sem("aux_done"), sem("aux_evac"), sem("w_ready")
        hT0_done, hT0_evac = sem("hT0_done"), sem("hT0_evac")
        pst_done, pst_evac, pst_stored = sem("pst_done"), sem("pst_evac"), sem("pst_stored")
        h0_loaded, h0_tr, h0T_evac = [sem("h0_loaded0"), sem("h0_loaded1")], sem("h0_tr"), sem("h0T_evac")
        y_mm, y_free, y_done, y_act = sem("y_mm"), sem("y_free"), sem("y_done"), sem("y_act")
        st_mm, hn_done, hn_stored = sem("st_mm"), sem("hn_done"), sem("hn_stored")
        dch = sem("dch")
        l_conv, l_mm, l_sig, l_la, l_at, l_w, l_s = (sem("l_conv"), sem("l_mm"), sem("l_sig"), sem("l_la"),
                                                     sem("l_at"), sem("l_w"), sem("l_s"))
        l_bank, l_gy, l_done = sem("l_bank"), sem("l_gy"), sem("l_done")
        rs_mm, rs_ms, rs_rt, rs_ok = sem("rs_mm"), sem("rs_ms"), sem("rs_rt"), sem("rs_ok")
        mix_mm, mix_sig, mix_done = sem("mix_mm"), sem("mix_sig"), sem("mix_done")
        x_again, wo_mm, wo_done = sem("x_again"), sem("wo_mm"), sem("wo_done")
        tails_T, tails_evac, tails_stored = sem("tails_T"), sem("tails_evac"), sem("tails_stored")

        xn2T = Y
        rr = Region(RH + 2600, 3544)
        w_r = v3(rr.take(KC * 36), KC)
        rbias = rr.take(36)
        L = v3(rr.take(NT * 36), NT)
        em, c1, oh1, oh2, Msel, rankm, em2 = (v3(rr.take(NT * NE), NT) for _ in range(7))
        goh = v3(rr.take(NT * EG), NT)
        ge = v3(rr.take(NT * EG), NT)
        ie32 = rr.take(NE)
        ir32 = rr.take(NE)
        rcol = v3(rr.take(24 * NT), 24)
        rrow = rr.take(16)
        npass_i = rr.take(2).bitcast(i32)
        ridx = rr.take(2 * NT).bitcast(i32)
        eweight = v3(rr.take(2 * NT), 2)
        pweight = v3(rr.take(2 * NT), 2)
        idx_all = rr.take(18).bitcast(i32)
        idx_cur = rr.take(1).bitcast(i32)
        tokid = rr.take(NT)
        tokid16 = rr.take(2).bitcast(fp16)
        rx = Region(RY, 6144)
        xg = rx.take(D)
        xe = v3(rx.take(KC * 128), KC)
        yrow = v3(rx.take(2 * 1024), 2)
        rq = Region(keep.at, 6144)
        pick = v3(rq.take(NT * 1024).bitcast(fp16), NT)
        hid = [v3(rq.take(FC * SLOTS), FC) for _ in range(2)]
        hsil = [v3(rq.take(FC * SLOTS), FC) for _ in range(2)]
        shifted = v3(rq.take(NT * NE), NT)
        pT = v3(arena[:, RH:RH + 2 * T], 2)
        p_in = v3(arena[:, RH + 2 * T:RH + 2 * T + NT * PLE], NT)
        w_ple_sb = v3(slot[2], 2)
        gsig = [arena[:, RH + 2048 + 256 * i:RH + 2304 + 256 * i] for i in range(2)]
        gfin = slot[3][:, 0:D]
        yfin = [slot[3][:, D:2 * D], slot[4][:, 0:D]]
        cg = [slot[0][:, 0:D], slot[1][:, 0:D]]

        router_in, r_mm, r_lt, r_exp, r_step = sem("router_in"), sem("r_mm"), sem("r_lt"), sem("r_exp"), sem("r_step")
        rank_mm, pass_ready, route_ready = sem("rank_mm"), sem("pass_ready"), sem("route_ready")
        xn_stored = sem("xn_stored")
        pick_ready, idx_mm, idx_ready, idx_used = sem("pick_ready"), sem("idx_mm"), sem("idx_ready"), sem("idx_used")
        gathered = sem("gathered")
        xe_tr, xe_evac = sem("xe_tr"), sem("xe_evac")
        ew_loaded = [sem(f"ew_loaded{s}") for s in range(6)]
        e_step = sem("e_step")
        gu_act, gu_done = sem("gu_act"), sem("gu_done")
        yrow_out = [sem("yrow_out0"), sem("yrow_out1")]
        mch, dn_free, p_loaded, ple_step, f_rc = sem("mch"), sem("dn_free"), sem("p_loaded"), sem("ple_step"), sem("f_rc")
        comb_in, comb_done = [sem("comb_in0"), sem("comb_in1")], sem("comb_done")
        ple_in, p_T, p_evac = sem("ple_in"), sem("p_T"), sem("p_evac")
        ple_mm, ple_sig, ple_done = sem("ple_mm"), sem("ple_sig"), sem("ple_done")
        pslab = [sem("pslab0"), sem("pslab1")]
        f_sq, f_ms, f_rt, f_ok = sem("f_sq"), sem("f_ms"), sem("f_rt"), sem("f_ok")
        f_out = [sem("f_out0"), sem("f_out1")]
        gfin_in = sem("gfin_in")

        w_in = a["w_in"]

        def cols(w, at):
            return w[0, :, ds(at, SLAB)].rearrange("(k p) c -> p k c", p=128)

        class Chain:
            def __init__(self, eng, s):
                self.eng, self.s, self.base, self.k = eng, s, 0, 0

            def __call__(self, ins):
                self.k += 1
                ins.then_inc(self.s, 1)
                self.eng.wait_ge(self.s, self.base + self.k)

            def loop(self, i, per):
                self.start = self.base + self.k
                self.base, self.k = self.start + i * per, 0

            def end(self, trips, per):
                assert self.k == per, self.k
                self.base, self.k = self.start + trips * per, 0

        def ridx_col(k, t):
            return ridx[:, k * NT + t:k * NT + t + 1]

        def spread(ap, n):
            return ap.unsqueeze(len(ap.shape)).broadcast_to(list(ap.shape) + [n])

        def spread_mid(ap, n):
            return ap.unsqueeze(1).broadcast_to([ap.shape[0], n] + list(ap.shape[1:]))

        def streams(ap):
            return ap[:, SEQ:T].rearrange("p (b t) -> p b t", t=SLEN)

        def pstreams(ap):
            return ap[:, S0:PADDED].rearrange("p (b t) -> p b t", t=SPAD)

        lru_rows = slot[5][:, 1536:1664]
        tail_rows = arena[0:27, 4 * SLABF:4 * SLABF + NCONV * 128]
        ss_c, ms_c, rt_c, rstd_c = 128, 140, 152, 164
        lam_s = 176

        wait_stop = sem("wait_stop")

        block = ctx.enter_context(nc.Block())

        @block.sync
        def _(sp):
            for t in range(NT):
                src = a["x_prompt"][0, t * 128:(t + 1) * 128, :] if t < 2 else a["x_sample"].rearrange("b s d -> (b s) d")
                sp.dma_start(x_in[:, t, :], src).then_inc(x_loaded, 16)
            sp.dma_start(w_dt, w_in[0, :, OFF_DT:OFF_DT + HEADS].rearrange("(k p) c -> p k c", p=128)).then_inc(dt_loaded, 16)

            def load_slab(parity, w, at, used, count):
                sp.wait_ge(used, count)
                sp.sem_inc(wait_stop, 1)
                sp.dma_start(slab[parity], cols(w, at)).then_inc(slab_loaded[parity], 16)

            with sp.Fori(0, GROUPS) as g:
                sp.wait_ge(dt_done, 1)
                sp.wait_ge(proj_done, 10 * g + 1)
                for n, off in enumerate((OFF_B, OFF_C)):
                    sp.dma_start(slab[2][:, :, n * 128:(n + 1) * 128],
                                 w_in[0, :, ds(g * NST + off, NST)].rearrange("(k p) c -> p k c", p=128)).then_inc(side_loaded, 16)
                load_slab(0, w_in, g * 512 + OFF_X, proj_done, 10 * g + 1)
                load_slab(1, w_in, g * 512 + OFF_X + SLAB, proj_done, 10 * g + 2)
                sp.wait_ge(cum_stored, 16)
                sp.wait_ge(dt_tr, 1)
                sp.wait_ge(y_done, 4 * g + 1)
                sp.wait_ge(y_mm, 4 * g + 1)
                sp.dma_start(decay, acum_d[ds(g * HPG, HPG), :].partition_broadcast(128)).then_inc(cum_loaded, 16)
                for half in range(2):
                    sp.dma_start(growth[half * 64:(half + 1) * 64, :, :],
                                 acum_d[ds(g * HPG, HPG), :].rearrange("(j h) t -> h j t", h=2)[half].partition_broadcast(64)
                                 ).then_inc(cum_loaded, 16)
                load_slab(0, w_in, g * 512 + OFF_Z, proj_done, 10 * g + 6)
                load_slab(1, w_in, g * 512 + OFF_Z + SLAB, proj_done, 10 * g + 8)
            with sp.Fori(0, GROUPS) as g:
                sp.wait_ge(proj_done, 34)
                sp.wait_ge(l_mm, 4 * g + 1)
                for n, name in enumerate(("w_lru_a", "w_lru_x")):
                    sp.dma_start(lw[:, 4 * n:4 * n + 4, :], a[name][0, ds(g * 4, 4), :, :].rearrange("n k j -> k n j")).then_inc(side_loaded, 16)
                load_slab(0, w_in, g * 512 + OFF_XL, proj_done, 8 * g + 40)
                load_slab(1, w_in, g * 512 + OFF_XL + SLAB, proj_done, 8 * g + 42)
                load_slab(0, w_in, g * 512 + OFF_GY, proj_done, 8 * g + 44)
                load_slab(1, w_in, g * 512 + OFF_GY + SLAB, proj_done, 8 * g + 46)
            sp.wait_ge(proj_done, 74)
            with sp.Fori(0, 8) as i:
                load_slab(0, w_in, i * SLAB + OFF_GM, mix_mm, 8 * i + 1)
                load_slab(1, a["w_out_m"], i * SLAB, mix_mm, 8 * i + 2)
                load_slab(0, w_in, i * SLAB + OFF_GR, mix_mm, 8 * i + 4)
                load_slab(1, a["w_out_r"], i * SLAB, mix_mm, 8 * i + 6)
            sp.wait_ge(mix_mm, 66)
            with sp.Fori(0, 4) as i:
                load_slab(0, a["w_o"], i * 512, wo_mm, 6 * i + 1)
                load_slab(1, a["w_o"], i * 512 + SLAB, wo_mm, 6 * i + 3)

            sp.wait_ge(pass_ready, 1)
            n_pass = sp.value_load(npass_i[0:1, 0:1], min_val=1, max_val=PASSES)
            sp.wait_ge(mix_done, KC + 2)
            sp.wait_ge(wo_mm, 27)
            sp.wait_ge(n_tr, 24)
            sp.wait_ge(xn_stored, NT * 16)
            sp.wait_ge(tails_stored, 96)
            with sp.Fori(0, n_pass) as p:
                sp.wait_ge(comb_done, p * (2 * NT) + 1)
                sp.sem_inc(wait_stop, 1)
                with sp.Fori(0, NE) as e:
                    for s in range(6):
                        sp.wait_ge(e_step, (p * NE + e) * 8 + (1, 2, 3, 4, 6, 8)[s])
                        if s < 4:
                            w = a["w_exp_gate" if s < 2 else "w_exp_up"]
                            src = w[0, ds(e, 1), (s % 2) * (D // 2):(s % 2 + 1) * (D // 2), :].rearrange("o (k p) c -> p (o k) c", p=128)
                            dst = v3(slot[s], KC // 2)
                        else:
                            src = a["w_exp_down"][0, ds(e, 1), :, (s - 4) * 1024:(s - 3) * 1024].rearrange("o (k p) c -> p (o k) c", p=128)
                            dst = v3(slot[s], FC)
                        sp.dma_start(dst, src).then_inc(ew_loaded[s], 16)
            sp.wait_ge(e_step, n_pass * (8 * NE) + 8)
            sp.dma_start(w_ple_sb, a["w_ple"][0].rearrange("(k p) c -> p k c", p=128)).then_inc(ple_in, 16)
            sp.dma_start(gfin, a["g_final"].partition_broadcast(128)).then_inc(gfin_in, 16)
            sp.wait_ge(comb_done, n_pass * (2 * NT) + 1)
            sp.sem_inc(wait_stop, 1)
            with sp.Fori(0, 4) as i:
                for s in range(2):
                    sp.wait_ge(ple_mm, 6 * i + 3 * s + 1)
                    sp.dma_start(slab[s], cols(a["w_ple_gate"], i * 512 + s * SLAB)).then_inc(pslab[s], 16)

        @block.gpsimd
        def _(pool):
            n = 0
            def rows(src, at, count):
                done = 0
                while done < count:
                    r = at + done
                    m = min(count - done, 128 - r % 128)
                    pool.dma_start(prow[r % 128:r % 128 + m, r // 128, :], src[done:done + m, :]).then_inc(params_in, 16)
                    done += m
                    nonlocal n
                    n += 1
            r16 = lambda ap: ap.rearrange("o (c p) -> (o c) p", p=128)
            pool.memset(slot[5][:, 0:384], 0.0).then_inc(consts_ready, 1)
            pool.wait_ge(consts_ready, 1)
            for name, at in (("g_mix", P_GMIX), ("g_ffn", P_GFFN), ("g_ple", P_GPLE), ("g_ssm", P_GSSM),
                             ("b_lru_a", P_BA), ("b_lru_x", P_BX), ("lru_lambda", P_LAM)):
                rows(r16(a[name]), at, 16)
            rows(r16(a["conv_m_b"]), P_CB, 24)
            rows(r16(a["conv_r_b"]), P_CB + 24, 16)
            rows(a["conv_m_w"].rearrange("o k (c p) -> (o k c) p", p=128), P_CW, 96)
            rows(a["conv_r_w"].rearrange("o k (c p) -> (o k c) p", p=128), P_CR, 64)
            assert n == PARAM_DMAS, n
            pool.memset(ident, 0.0).then_inc(consts_ready, 1)
            pool.memset(ones, 1.0).then_inc(consts_ready, 1)
            pool.memset(convmem[:, :, 0:HIST], 0.0).then_inc(consts_ready, 1)
            pool.wait_ge(consts_ready, 4)
            pool.affine_select(out=ident, in_=ident, compare_op=ALU.not_equal, fill=1.0, base=0,
                               pattern=[[-1, 128]], channel_multiplier=1).then_inc(consts_ready, 1)
            pool.affine_select(out=before, in_=ones, compare_op=ALU.is_gt, fill=0.0, base=0,
                               pattern=[[1, 128]], channel_multiplier=-1).then_inc(consts_ready, 1)
            pool.affine_select(out=causal[:, 0, :], in_=ones, compare_op=ALU.is_ge, fill=0.0, base=0,
                               pattern=[[1, 128]], channel_multiplier=-1).then_inc(consts_ready, 1)
            pool.affine_select(out=stream_of, in_=ones[:, 0:NSEQ], compare_op=ALU.is_ge, fill=0.0, base=0,
                               pattern=[[-SLEN, NSEQ]], channel_multiplier=1).then_inc(consts_ready, 1)
            pool.wait_ge(consts_ready, 8)
            pool.affine_select(out=stream_of, in_=stream_of, compare_op=ALU.is_ge, fill=0.0, base=SLEN - 1,
                               pattern=[[SLEN, NSEQ]], channel_multiplier=-1).then_inc(consts_ready, 1)
            pool.affine_select(out=v3(causal[:, 1, :], NSEQ), in_=v3(causal[:, 0, :], NSEQ), compare_op=ALU.is_ge,
                               fill=0.0, base=0, pattern=[[-SLEN, NSEQ], [0, SLEN]], channel_multiplier=1).then_inc(consts_ready, 1)
            pool.memset(rmask, 1.0).then_inc(consts_ready, 1)
            pool.wait_ge(consts_ready, 11)
            pool.memset(rmask[:, 0:SEQ].rearrange("p (c t) -> p c t", t=128)[:, :, 0:1], 0.0).then_inc(consts_ready, 1)
            pool.memset(rmask[:, SEQ:T].rearrange("p (c t) -> p c t", t=SLEN)[:, :, 0:1], 0.0).then_inc(consts_ready, 1)
            pool.iota(iota64, pattern=[[1, 64]], base=0, channel_multiplier=0, allow_small_or_imprecise_dtypes=True).then_inc(consts_ready, 1)
            assert CONSTS == 14
            pool.dma_start(hist_rows[:, 0:XBC], a["state_ssm_conv"][0].rearrange("b k c -> (b k) c")).then_inc(setup_in, 16)
            pool.dma_start(hist_rows[:, XBC:XBC + D], a["state_lru_conv"][0].rearrange("b k c -> (b k) c")).then_inc(setup_in, 16)
            pool.dma_start(sm[:, 0:128], a["state_lru"][0].rearrange("b (c p) -> (b c) p", p=128)).then_inc(setup_in, 16)
            pool.dma_start(dcol[:, 0:1], a["dt_bias"].rearrange("o h -> h o")).then_inc(setup_in, 16)
            pool.dma_start(dcol[:, 1:2], a["a_log"].rearrange("o h -> h o")).then_inc(setup_in, 16)
            for half in range(2):
                pool.dma_start(dskip[half * 64:(half + 1) * 64, :],
                               a["d_skip"][0].rearrange("(c h) -> h c", h=2)[half].partition_broadcast(64),
                               allow_slow_non_contiguous=True).then_inc(setup_in, 16)
            pool.wait_ge(dt_step, 3)
            pool.dma_start(acum_d, cumT).then_inc(cum_stored, 16)

            def load_h0(jj, parity):
                pool.dma_start(h0[parity], a["state_ssm"][0].rearrange("b (c h) p n -> (h p) c b n", h=2)[:, ds(jj, 1)].rearrange("q o b n -> q (o b) n")
                               ).then_inc(h0_loaded[parity], 16)
            pool.wait_ge(dt_tr, 1)
            for j in range(2):
                load_h0(j, j)

            def store_h(jj, parity):
                pool.wait_ge(hn_done, jj + 2)
                pool.dma_start(ssm_s[0].rearrange("b (c h) p n -> (h p) c b n", h=2)[:, ds(jj, 1)].rearrange("q o b n -> q (o b) n"),
                               h0[parity]).then_inc(hn_stored, 16)
                pool.wait_ge(hn_stored, jj * 16 + 16)

            with pool.Fori(0, KC // 2 - 1) as i:
                for j in range(2):
                    store_h(2 * i + j, j)
                    load_h0(2 * i + j + 2, j)
            for jj in (KC - 2, KC - 1):
                store_h(jj, jj % 2)
            pool.wait_ge(mix_mm, 4 * KC + 2)
            pool.wait_ge(tails_T, 11)
            for t in range(NT):
                src = a["x_prompt"][0, t * 128:(t + 1) * 128, :] if t < 2 else a["x_sample"].rearrange("b s d -> (b s) d")
                pool.dma_start(x_res[:, t, :], src).then_inc(x_again, 16)
            pool.dma_start(w_r[:, :, 0:EG], a["w_router_group"][0].rearrange("(k p) c -> p k c", p=128)).then_inc(router_in, 16)
            pool.dma_start(w_r[:, :, EG:36], a["w_router_expert"][0].rearrange("(k p) c -> p k c", p=128)).then_inc(router_in, 16)
            pool.dma_start(rbias[:, 0:EG], a["b_router_group"][0].partition_broadcast(128)).then_inc(router_in, 16)
            pool.dma_start(rbias[:, EG:36], a["b_router_expert"][0].partition_broadcast(128)).then_inc(router_in, 16)
            pool.iota(ie32, pattern=[[1, NE]], base=0, channel_multiplier=0, allow_small_or_imprecise_dtypes=True).then_inc(consts_ready, 1)
            pool.iota(ir32, pattern=[[-1, NE]], base=100, channel_multiplier=0, allow_small_or_imprecise_dtypes=True).then_inc(consts_ready, 1)
            pool.iota(tokid, pattern=[[128, NT]], base=0, channel_multiplier=1, allow_small_or_imprecise_dtypes=True).then_inc(consts_ready, 1)
            for t in range(NT):
                pool.wait_ge(n_scaled, NT + t + 1)
                pool.dma_start(xn_d[t * 128:(t + 1) * 128, :], nrm[(NT + t) % 2]).then_inc(xn_stored, 16)
                pool.wait_ge(xn_stored, 16 * t + 16)
            pool.wait_ge(pass_ready, 1)
            n_pass = pool.value_load(npass_i[0:1, 0:1], min_val=1, max_val=PASSES)
            with pool.Fori(0, n_pass) as p:
                with pool.Fori(0, PAIRS + 1) as q:
                    n = p * (PAIRS + 1) + q
                    pool.wait_ge(idx_ready, n + 1)
                    pool.wait_ge(xe_tr, n * 4 + 1)
                    pool.sem_inc(wait_stop, 1)
                    pool.indirect_dma_start(out=xg, out_offset=None, in_=xn_d[:, :],
                                            in_offset=bass.IndirectOffsetOnAxis(ap=idx_cur[:, 0:1], axis=0)).then_inc(gathered, 16)
                for h in range(2):
                    pool.wait_ge(yrow_out[h], p * (16 * NE) + 16 * NE + 1)
                pool.wait_ge(e_step, p * (8 * NE) + 8 * NE + 8)
                for n in range(2 * NT):
                    pool.wait_ge(comb_done, p * (2 * NT) + max(n - 1, 0) + 1)
                    pool.sem_inc(wait_stop, 1)
                    pool.indirect_dma_start(out=cg[n % 2], out_offset=None, in_=y_d[:, :],
                                            in_offset=bass.IndirectOffsetOnAxis(ap=ridx_col(n % 2, n // 2), axis=0)).then_inc(comb_in[n % 2], 16)
            for t in range(NT):
                src = a["p_prompt"][0, 0, t * 128:(t + 1) * 128, :] if t < 2 else a["p_sample"][0].rearrange("b s d -> (b s) d")
                pool.dma_start(p_in[:, t, :], src).then_inc(p_loaded, 16)

        @block.scalar
        def _(act):
            A = nc.scalar.activation
            for started in (pst_stored, gu_act, *yrow_out):
                act.sem_inc(started, 1)
            act.sem_inc(proj_free, 2)
            act.sem_inc(silu_done, 2)
            act.sem_inc(dn_free, 2)
            act.sem_inc(l_sig, 2)

            def square_tile(n, src):
                if n >= 2:
                    act.wait_ge(n_tr, 4 * (n - 1))
                if n >= 5:
                    act.wait_ge(xn_stored, 16 * min(n - 4, NT))
                A(nrm[n % 2], src, ACT.Square, accum_out=sm[:, ss_c + n:ss_c + n + 1]).then_inc(n_sq, 1)
                act.wait_ge(n_ms, n + 1)
                A(sm[:, rt_c + n:rt_c + n + 1], sm[:, ms_c + n:ms_c + n + 1], ACT.Sqrt).then_inc(n_rt, 1)

            for t in range(NT):
                act.wait_ge(x_loaded, 16 * NT)
                square_tile(t, x_in[:, t, :])
            act.wait_ge(consts_ready, CONSTS)
            for b in range(2):
                act.wait_ge(hist_T, b + 1)
                A(convmem[:, 20 * b:20 * b + 20, HIST:27], v3(banks[4 + b][:, 0:480], 20), ACT.Copy).then_inc(hist_evac, 1)
            act.wait_ge(hist_T, 3)
            A(lru_h0, v3(banks[7][:, 0:128], NSEQ), ACT.Copy).then_inc(hist_evac, 1)
            act.wait_ge(setup_in, 16 * 7)
            act.wait_ge(dt_step, 1)
            A(dA, dtmp2, ACT.Exp).then_inc(dt_act, 1)
            A(dcol[:, 2:3], dcol[:, 1:2], ACT.Exp).then_inc(dt_act, 1)
            act.wait_ge(dt_step, 2)
            A(ddT, cumT, ACT.Ln).then_inc(dt_act, 1)
            act.wait_ge(dt_step, 4)
            A(ddT, ddT, ACT.Exp).then_inc(dt_act, 1)
            A(dcol[:, 4:5], cumT[:, SEQ - 1:SEQ], ACT.Exp).then_inc(dt_act, 1)
            act.wait_ge(dt_step, 6)
            A(sm[:, lam_s + 16:lam_s + 32], sm[:, lam_s:lam_s + 16], ACT.Exp).then_inc(dt_act, 1)
            act.wait_ge(dt_step, 7)
            A(sm[:, lam_s + 48:lam_s + 64], sm[:, lam_s + 32:lam_s + 48], ACT.Ln).then_inc(dt_act, 1)

            def to_padded(n, nconv, m):
                act.wait_ge(proj_done, n + 3)
                act.wait_ge(conv_done, nconv + 1)
                bank, r = banks[m % 2], raw[m % 2]
                A(r[:, HIST:S0], bank[:, 0:SEQ], ACT.Copy)
                A(pstreams(r)[:, :, HIST:SPAD], streams(bank[:, 0:T]), ACT.Copy).then_inc(proj_free, 1)

            with act.Fori(0, GROUPS) as g:
                conv_out = [BT, CT] + [xsT[:, j, :] for j in range(4)]

                def silu(m):
                    act.wait_ge(conv_done, 6 * g + m + 3)
                    c = acc[m % 2]
                    A(conv_out[m][:, 0:SEQ], c[:, 0:SEQ], ACT.Silu)
                    A(streams(conv_out[m]), pstreams(c)[:, :, 0:SLEN], ACT.Silu).then_inc(silu_done, 1)

                act.wait_ge(y_done, 4 * g + 1)
                for m in range(6):
                    to_padded(10 * g + m, 6 * g + m, m)
                    if m:
                        silu(m - 1)
                silu(5)
                for m in range(6, 10):
                    act.wait_ge(proj_done, 10 * g + m + 3)
                    A(Y[:, 4 * g + m - 6, :], banks[m % 2][:, 0:T], ACT.Silu).then_inc(proj_free, 1)
                    if m == 7:
                        act.wait_ge(seg_ready, g + 1)
                        A(decay, decay, ACT.Exp)
                        A(growth, growth, ACT.Exp).then_inc(exp_done, 1)
                act.wait_ge(hT0_done, g + 1)
                A(hT0, banks[7][:, :], ACT.Copy).then_inc(hT0_evac, 1)
                act.wait_ge(pst_done, g + 1)
                act.wait_ge(pst_stored, 16 * g + 1)
                A(pst, v3(banks[3][:, :], 4), ACT.Copy).then_inc(pst_evac, 1)
                act.wait_ge(pst_evac, g + 1)
                act.dma_start(ssm_p[0, 0].rearrange("(c h) p n -> (h p) c n", h=2)[:, ds(4 * g, 4), :], pst).then_inc(pst_stored, 16)
                for j in range(4):
                    act.wait_ge(h0_tr, 4 * g + j + 1)
                    act.wait_ge(y_mm, 4 * g + j + 1)
                    A(h0T[:, 0:4, :], v3(banks[2][:, :], 4), ACT.Copy)
                    A(h0T[:, 4:8, :], v3(banks[3][:, :], 4), ACT.Copy).then_inc(h0T_evac, 1)
                    act.wait_ge(y_done, 4 * g + j + 2)
                    A(ysq[j % 2], ytmp[j % 2], ACT.Square)
                    A(Y[:, 4 * g + j, :], ytmp[j % 2], ACT.Identity, scale=pcol[:, ds(4 * g + j + P_GSSM, 1)]).then_inc(y_act, 1)

            with act.Fori(0, GROUPS) as g:
                for m in range(4):
                    to_padded(8 * g + m + 40, 4 * g + m + 24, m)
                act.wait_ge(l_done, g + 1)
                for m in range(4, 8):
                    act.wait_ge(proj_done, 8 * g + m + 43)
                    A(gy[:, m - 4, :], banks[m % 2][:, 0:T], ACT.Gelu_apprx_tanh).then_inc(proj_free, 1)
                for m in range(4):
                    act.wait_ge(l_mm, 4 * g + m + 2)
                    b = 2 + 2 * (m % 2)
                    A(lr[:, m, :], banks[b][:, 0:T], ACT.Sigmoid, bias=pcol[:, ds(4 * g + m + P_BA, 1)])
                    A(li[:, m, :], banks[b + 1][:, 0:T], ACT.Sigmoid, bias=pcol[:, ds(4 * g + m + P_BX, 1)]).then_inc(l_sig, 1)
                act.wait_ge(l_la, g + 1)
                A(lr, la_, ACT.Exp)
                A(lt, la_, ACT.Tanh).then_inc(l_at, 1)
                act.wait_ge(l_w, g + 1)
                A(la_, lt, ACT.Sqrt).then_inc(l_s, 1)

            for q in range(10):
                act.wait_ge(tails_T, q + 1)
                A(tail_rows[:, 512 * q:512 * q + 512], banks[6 + q % 2][0:27, :], ACT.Copy).then_inc(tails_evac, 1)
            act.wait_ge(tails_T, 11)
            A(sm[0:16, 0:128], banks[6][0:16, 0:128], ACT.Copy).then_inc(tails_evac, 1)
            A(lru_rows, banks[6][:, 128:256], ACT.Copy).then_inc(tails_evac, 1)
            act.wait_ge(tails_evac, 12)
            act.dma_start(sconv_p[0, 0], tail_rows[0:3, 0:XBC]).then_inc(tails_stored, 16)
            act.dma_start(lconv_p[0, 0], tail_rows[0:3, XBC:XBC + D]).then_inc(tails_stored, 16)
            act.dma_start(sconv_s[0].rearrange("b k c -> (b k) c"), tail_rows[3:27, 0:XBC]).then_inc(tails_stored, 16)
            act.dma_start(lconv_s[0].rearrange("b k c -> (b k) c"), tail_rows[3:27, XBC:XBC + D]).then_inc(tails_stored, 16)
            act.dma_start(lru_p[0, 0].rearrange("(c p) -> c p", p=128), sm[0:16, 0:128]).then_inc(tails_stored, 16)
            act.dma_start(lru_s[0].rearrange("b (c p) -> (b c) p", p=128), lru_rows).then_inc(tails_stored, 16)
            act.wait_ge(rs_ms, 1)
            A(rstdB, rstdB, ACT.Sqrt).then_inc(rs_rt, 1)

            with act.Fori(0, 8) as i:
                for src, dst in ((0, sg_m), (2, sg_r)):
                    for cc in range(2):
                        act.wait_ge(mix_mm, 8 * i + 2 * src + cc + 3)
                        act.wait_ge(mix_done, 2 * i + cc + 1)
                        A(dst[cc], banks[2 * src + cc][:, 0:T], ACT.Sigmoid).then_inc(mix_sig, 1)

            act.wait_ge(tails_stored, 96)
            for t in range(NT):
                act.wait_ge(wo_done, 24 + 6)
                square_tile(NT + t, x_res[:, t, :])
            act.wait_ge(r_lt, 1)
            A(ge, ge, ACT.Exp).then_inc(r_exp, 1)
            act.wait_ge(r_lt, 2)
            A(rcol[:, 8, :], rcol[:, 8, :], ACT.Exp).then_inc(r_exp, 1)

            act.wait_ge(pass_ready, 1)
            n_pass = act.value_load(npass_i[0:1, 0:1], min_val=1, max_val=PASSES)
            with act.Fori(0, n_pass) as p:
                act.wait_ge(comb_done, p * (2 * NT) + 1)
                with act.Fori(0, PAIRS) as q:
                    for x in range(2):
                        E = p * NE + 2 * q + x
                        act.wait_ge(e_step, 8 * E + 8 + 2)
                        act.wait_ge(gu_done, E + 1)
                        A(hsil[x], v3(banks[2 * x][:, 0:256], FC), ACT.Silu).then_inc(gu_act, 1)
                        for b in range(4):
                            act.wait_ge(e_step, 8 * E + 8 + 5 + b)
                            if b % 2 == 0:
                                act.wait_ge(yrow_out[b // 2], 16 * E + 1)
                            A(yrow[0:SLOTS, b // 2, (b % 2) * 512:(b % 2) * 512 + 512], banks[6 + b % 2][0:SLOTS, :], ACT.Copy).then_inc(dn_free, 1)
                            if b % 2 == 1:
                                act.wait_ge(dn_free, 4 * E + b + 3)
                                act.dma_start(y_d[ds((2 * q + x) * SLOTS, SLOTS), (b // 2) * 1024:(b // 2 + 1) * 1024],
                                              yrow[0:SLOTS, b // 2, :]).then_inc(yrow_out[b // 2], 16)

            for t in range(NT):
                act.wait_ge(comb_done, n_pass * (2 * NT) + 1)
                square_tile(2 * NT + t, x_res[:, t, :])
            act.wait_ge(p_T, 1)
            A(pT[:, 0, :], banks[4][:, 0:T], ACT.Copy).then_inc(p_evac, 1)
            A(pT[:, 1, :], banks[5][:, 0:T], ACT.Copy).then_inc(p_evac, 1)
            with act.Fori(0, 4) as i:
                for n in range(6):
                    act.wait_ge(ple_mm, 6 * i + n + 4)
                    act.wait_ge(ple_done, 6 * i + n + 5)
                    A(gsig[n % 2], banks[n][:, 0:SLAB], ACT.Sigmoid).then_inc(ple_sig, 1)
            for t in range(NT):
                act.wait_ge(ple_done, 24 + 6)
                if t >= 2:
                    act.wait_ge(f_out[t % 2], 16)
                else:
                    act.wait_ge(gfin_in, 16)
                A(yfin[t % 2], x_res[:, t, :], ACT.Square, accum_out=sm[:, t:t + 1]).then_inc(f_sq, 1)
                act.wait_ge(f_ms, t + 1)
                A(sm[:, 8 + t:9 + t], sm[:, 4 + t:5 + t], ACT.Sqrt).then_inc(f_rt, 1)
                act.wait_ge(f_ok, t + 1)
                dst = y_p[0, t * 128:(t + 1) * 128, :] if t < 2 else y_s.rearrange("b s d -> (b s) d")
                act.dma_start(dst, yfin[t % 2]).then_inc(f_out[t % 2], 16)
            act.wait_ge(f_out[0], 32)
            act.wait_ge(f_out[1], 16)
            act.wait_ge(tails_stored, 96)
            act.wait_ge(pst_stored, 16 * GROUPS + 1)
            act.wait_ge(hn_stored, 16 * KC)

        @block.vector
        def _(dve):
            V = nc.vector
            link = Chain(dve, dch)
            TT, TS, STT = V.tensor_tensor, V.tensor_scalar, V.scalar_tensor_tensor
            for started in (y_done, hn_done, l_done, comb_done, gu_done):
                dve.sem_inc(started, 1)
            dve.sem_inc(conv_done, 2)
            dve.sem_inc(n_evac, 4)
            dve.sem_inc(y_free, 1)
            dve.sem_inc(mix_done, 2)
            dve.sem_inc(wo_done, 6)
            dve.sem_inc(ple_done, 6)
            V.memset(ss_acc, 0.0)

            def norm_tile(n, src, gain, dst, t):
                dve.wait_ge(n_sq, n + 1)
                TS(sm[:, ms_c + n:ms_c + n + 1], sm[:, ss_c + n:ss_c + n + 1], 1.0 / D, EPS, ALU.mult, ALU.add).then_inc(n_ms, 1)
                dve.wait_ge(n_rt, n + 1)
                rstd = sm[:, rstd_c + n:rstd_c + n + 1]
                link(V.reciprocal(rstd, sm[:, rt_c + n:rt_c + n + 1]))
                TS(nrm[n % 2], src, rstd, None, ALU.mult).then_inc(n_scaled, 1)
                for b in range(4):
                    dve.wait_ge(n_tr, 4 * n + b + 1)
                    TT(dst[:, 4 * b:4 * b + 4, t * 128:(t + 1) * 128], v3(banks[b][:, :], 4),
                       spread(pcol[:, gain + 4 * b:gain + 4 * b + 4], 128), ALU.mult).then_inc(n_evac, 1)

            dve.wait_ge(ptr_done, 1)
            link(V.tensor_copy(pcol, banks[6][:, 0:384]))
            for t in range(NT):
                norm_tile(t, x_in[:, t, :], P_GMIX, xnT, t)

            dve.wait_ge(dt_done, 1)
            dve.wait_ge(setup_in, 16 * 7)
            dve.wait_ge(consts_ready, CONSTS)
            link(TS(dtmp, banks[4][0:HEADS, 0:T], dcol[:, 0:1], None, ALU.add))
            STT(dtmp2, dtmp, -1.0, dtmp, ALU.mult, ALU.min).then_inc(dt_step, 1)
            dve.wait_ge(dt_act, 2)
            TS(cumT, dA, 1.0, None, ALU.add).then_inc(dt_step, 1)
            dve.wait_ge(dt_act, 3)
            link(TS(cumT, cumT, 1.0, 1e-30, ALU.subtract, ALU.max))
            link(V.reciprocal(cumT, cumT))
            link(TT(dA, dA, cumT, ALU.mult))
            link(TT(ddT, ddT, dA, ALU.mult))
            link(STT(dtT, dtmp, 0.0, ddT, ALU.max, ALU.add))
            link(TS(dcol[:, 3:4], dcol[:, 2:3], -1.0, None, ALU.mult))
            link(TS(dA, dtT, dcol[:, 3:4], None, ALU.mult))
            V.tensor_tensor_scan(cumT, rmask, dA, 0.0, ALU.mult, ALU.add).then_inc(dt_step, 1)
            dve.wait_ge(dt_step, 3)
            for lo, hi, ln in ((0, SEQ, 128), (SEQ, T, SLEN)):
                seg = cumT[:, lo:hi].rearrange("p (c t) -> p c t", t=ln)
                last = TT(ddT[:, lo:hi].rearrange("p (c t) -> p c t", t=ln),
                          seg[:, :, ln - 1:ln].broadcast_to([HEADS, (hi - lo) // ln, ln]), seg, ALU.subtract)
            last.then_inc(dt_step, 1)
            dve.wait_ge(dt_act, 5)
            link(TT(ddT, ddT, dtT, ALU.mult))
            TS(ddfT, ddT[:, 0:128], dcol[:, 4:5], None, ALU.mult).then_inc(dt_step, 1)
            lam = pcol[:, P_LAM:P_LAM + 16]
            l0, l1, l2, l3 = (sm[:, lam_s + 16 * i:lam_s + 16 * i + 16] for i in range(4))
            STT(l0, lam, -1.0, lam, ALU.mult, ALU.min).then_inc(dt_step, 1)
            dve.wait_ge(dt_act, 6)
            TS(l2, l1, 1.0, None, ALU.add).then_inc(dt_step, 1)
            dve.wait_ge(dt_act, 7)
            link(TS(l2, l2, 1.0, 1e-30, ALU.subtract, ALU.max))
            link(V.reciprocal(l2, l2))
            link(TT(l1, l1, l2, ALU.mult))
            link(TT(l3, l3, l1, ALU.mult))
            link(TS(l0, lam, -1.0, 0.0, ALU.mult, ALU.max))
            link(TT(l0, l0, l3, ALU.add))
            link(TS(lam_c, l0, -8.0, None, ALU.mult))
            dve.wait_ge(dt_tr, 1)
            link(V.tensor_copy(tokcol, v3(banks[5][:, 0:320], 10)))

            def conv(nproj, nconv, m, c, tap, out):
                r, o = raw[m % 2], acc[m % 2]
                V.tensor_copy(r[:, 0:HIST], convmem[:, c, 0:HIST])
                link(V.tensor_copy(pstreams(r)[:, :, 0:HIST], convmem[:, c, HIST:27].rearrange("p (b t) -> p b t", t=HIST)))
                dve.wait_ge(proj_free, nproj + 3)
                if out is None:
                    dve.wait_ge(silu_done, nconv + 1)
                op = TS(o[:, 0:CONV], r[:, 0:CONV], tap(0), pcol[:, ds(c + P_CB, 1)], ALU.mult, ALU.add)
                V.tensor_copy(convmem[:, c, 0:HIST], r[:, SEQ:S0])
                V.tensor_copy(convmem[:, c, HIST:27].rearrange("p (b t) -> p b t", t=HIST), pstreams(r)[:, :, SLEN:SPAD])
                link(op)
                for k in range(1, TAPS - 1):
                    link(STT(o[:, 0:CONV], r[:, k:k + CONV], tap(k), o[:, 0:CONV], ALU.mult, ALU.add))
                k = TAPS - 1
                if out is None:
                    STT(o[:, 0:CONV], r[:, k:k + CONV], tap(k), o[:, 0:CONV], ALU.mult, ALU.add).then_inc(conv_done, 1)
                else:
                    STT(out[:, 0:SEQ], r[:, k:k + SEQ], tap(k), o[:, 0:SEQ], ALU.mult, ALU.add)
                    STT(streams(out), pstreams(r)[:, :, HIST:SPAD], tap(k), pstreams(o)[:, :, 0:SLEN], ALU.mult, ALU.add).then_inc(conv_done, 1)

            with dve.Fori(0, GROUPS) as g:
                link.loop(g, SSD_LINKS)
                dve.wait_ge(cum_loaded, 48 * g + 48)
                for t in range(NT):
                    d = decay[:, :, t * 128:(t + 1) * 128]
                    op = TT(d, d, spread(tokcol[:, C_CUM + t, ds(g * HPG, HPG)], 128), ALU.subtract)
                    op = link(op)
                TS(decay, decay, 0.0, None, ALU.min).then_inc(seg_ready, 1)
                for m in range(6):
                    c = (g + 16, g + 20, 4 * g, 4 * g + 1, 4 * g + 2, 4 * g + 3)[m]
                    conv(10 * g + m, 6 * g + m, m, c, lambda k: pcol[:, ds(c + (P_CW + 24 * k), 1)], None)
                dve.wait_ge(aux_done, 5 * g + 1)
                TT(cbm[:, 0:2, :], v3(banks[2][:, 0:256], 2), spread_mid(causal[:, 0, :], 2), ALU.mult)
                link(TT(cbm[:, 2, :], banks[2][:, 256:384], causal[:, 1, :], ALU.mult))
                dve.wait_ge(aux_done, 5 * g + 2)
                link(V.tensor_copy(Btok, v3(banks[3][:, 0:384], 3)))
                link(TT(Bseg, spread_mid(Btok[:, 2, :], NSEQ), spread(stream_of, NST), ALU.mult))
                for t in range(NT):
                    dve.wait_ge(aux_done, 5 * g + 3 + t)
                    bank = v3(banks[4 + t][:, :], HPG)
                    kinds = [(x_dt[:, t, :], C_DT + t), (x_dd[:, t, :], C_DD + t)] + [(x_ddf, C_DDF)] * (t == 0)
                    for dst, col in kinds:
                        last = TT(v3(dst, HPG), bank, spread(tokcol[:, col, ds(g * HPG, HPG)], HP), ALU.mult)
                    last.then_inc(aux_evac, 1)
                dve.wait_ge(exp_done, g + 1)
                for t in range(NT):
                    d = decay[:, :, t * 128:(t + 1) * 128]
                    last = TT(d, d, spread_mid(cbm[:, t, :], HPG), ALU.mult)
                last.then_inc(w_ready, 1)
                for j in range(4):
                    yt, gr = ytmp[j % 2], growth[:, j, :]
                    dve.wait_ge(y_mm, 4 * g + j + 2)
                    link(V.tensor_copy(dec, gr[:, SEQ + SLEN - 1:T:SLEN]))
                    link(TT(gr[:, 128:T], gr[:, 128:T], banks[4][:, 128:T], ALU.mult))
                    op = STT(yt, xsT[:, j, :], dskip[:, ds(4 * g + j, 1)], banks[5][:, 0:T], ALU.mult, ALU.add)
                    op.then_inc(y_free, 1)
                    dve.wait_ge(y_free, 4 * g + j + 2)
                    link(TT(yt[:, 128:T], yt[:, 128:T], gr[:, 128:T], ALU.add))
                    TT(yt, yt, Y[:, 4 * g + j, :], ALU.mult).then_inc(y_done, 1)
                    hb = h0[j % 2]
                    dve.wait_ge(st_mm, 4 * g + j + 1)
                    link(TT(hb, hb, spread(dec, NST), ALU.mult))
                    TT(hb[:, 0:4, :], hb[:, 0:4, :], v3(banks[6][:, :], 4), ALU.add)
                    TT(hb[:, 4:8, :], hb[:, 4:8, :], v3(banks[7][:, :], 4), ALU.add).then_inc(hn_done, 1)
                    dve.wait_ge(y_act, 4 * g + j + 1)
                    link(TT(ss_acc, ss_acc, ysq[j % 2], ALU.add))
                link.end(GROUPS, SSD_LINKS)

            dve.wait_ge(hn_stored, 16 * KC)
            dve.wait_ge(pst_stored, 16 * GROUPS + 1)
            with dve.Fori(0, GROUPS) as g:
                link.loop(g, LRU_LINKS)
                for m in range(4):
                    c = 4 * g + m + 24
                    conv(8 * g + m + 40, 4 * g + m + 24, m, c, lambda k: pcol[:, ds(4 * g + m + (P_CR + 16 * k), 1)], xl[:, m, :])
                dve.wait_ge(l_sig, 4 * g + 4 + 2)
                for m in range(4):
                    last = TS(la_[:, m, :], lr[:, m, :], lam_c[:, ds(4 * g + m, 1)], None, ALU.mult)
                last.then_inc(l_la, 1)
                link(TT(li, li, xl, ALU.mult))
                dve.wait_ge(l_at, g + 1)
                link(TS(la_, lt, -1.0, 1.0, ALU.mult, ALU.add))
                link(V.reciprocal(la_, la_))
                STT(lt, lt, -2.0, la_, ALU.mult, ALU.mult).then_inc(l_w, 1)
                dve.wait_ge(l_s, g + 1)
                link(TT(li, li, la_, ALU.mult))
                first = slice(SEQ, T, SLEN)
                h_in = v3(lt[:, 0, 0:32], 4)
                link(TT(h_in, lr[:, :, first], lru_h0[:, :, ds(4 * g, 4)].rearrange("p b m -> p m b"), ALU.mult))
                link(TT(li[:, :, first], li[:, :, first], h_in, ALU.add))
                link(V.memset(lr[:, :, first], 0.0))
                for m in range(4):
                    last = V.tensor_tensor_scan(la_[:, m, :], lr[:, m, :], li[:, m, :], 0.0, ALU.mult, ALU.add)
                link(last)
                V.tensor_copy(lru_end[:, 0, ds(4 * g, 4)], la_[:, :, SEQ - 1])
                V.tensor_copy(lru_end[:, 1:9, ds(4 * g, 4)].rearrange("p b m -> p m b"), la_[:, :, SEQ + SLEN - 1:T:SLEN])
                dve.wait_ge(proj_free, 8 * g + 8 + 40 + 2)
                TT(H[:, ds(4 * g, 4), :], la_, gy, ALU.mult).then_inc(l_done, 1)
                link.end(GROUPS, LRU_LINKS)

            dve.wait_ge(rs_mm, 1)
            TS(rstdB, banks[5][:, 0:T], 1.0 / D, EPS, ALU.mult, ALU.add).then_inc(rs_ms, 1)
            dve.wait_ge(rs_rt, 1)
            link(V.reciprocal(rstdB, rstdB))

            with dve.Fori(0, 8) as i:
                link.loop(i, 6)
                for cc in range(2):
                    dve.wait_ge(mix_mm, 8 * i + 2 + cc + 3)
                    link(TT(t_m[cc], rstdB, banks[2 + cc][:, 0:T], ALU.mult))
                    dve.wait_ge(mix_sig, 4 * i + cc + 1)
                    link(TT(t_m[cc], t_m[cc], sg_m[cc], ALU.mult))
                for cc in range(2):
                    dve.wait_ge(mix_mm, 8 * i + 6 + cc + 3)
                    dve.wait_ge(mix_sig, 4 * i + 2 + cc + 1)
                    link(TT(t_r[cc], sg_r[cc], banks[6 + cc][:, 0:T], ALU.mult))
                    TT(mixed[:, 2 * i + cc, :], t_m[cc], t_r[cc], ALU.add).then_inc(mix_done, 1)
                link.end(8, 6)
            dve.wait_ge(x_again, 16 * NT)
            with dve.Fori(0, 4) as i:
                for n in range(6):
                    dve.wait_ge(wo_mm, 6 * i + n + 4)
                    xr = x_res[:, n % 3, ds(i * 512 + (n // 3) * SLAB, SLAB)]
                    TT(xr, xr, banks[n][:, 0:SLAB], ALU.add).then_inc(wo_done, 1)
            dve.wait_ge(wo_done, 24 + 6)
            for t in range(NT):
                norm_tile(NT + t, x_res[:, t, :], P_GFFN, xn2T, t)

            dve.wait_ge(router_in, 64)
            dve.wait_ge(consts_ready, CONSTS + 3)
            dve.wait_ge(r_mm, 1)
            R = lambda c: rcol[:, c, :]
            link(TT(L, v3(banks[4][:, 0:NT * 36], NT), spread_mid(rbias, NT), ALU.add))
            gl, el = L[:, :, 0:EG], L[:, :, EG:36]
            link(V.tensor_reduce(R(0), gl, AX.X, ALU.max))
            TT(ge, gl, spread(R(0), EG), ALU.subtract).then_inc(r_lt, 1)
            dve.wait_ge(r_lt, 1)
            link(TT(goh, gl, spread(R(0), EG), ALU.is_equal))
            link(TT(goh, goh, spread_mid(ir32[:, 0:EG], NT), ALU.mult))
            link(V.tensor_reduce(R(3), goh, AX.X, ALU.max))
            link(TT(goh, goh, spread(R(3), EG), ALU.is_equal))
            dve.wait_ge(r_exp, 1)
            link(V.tensor_reduce(R(1), ge, AX.X, ALU.add))
            link(V.reciprocal(R(2), R(1)))
            link(TS(goh, goh, 1.0, BIG, ALU.subtract, ALU.mult))
            for t in range(NT):
                op = TT(v3(em[:, t, :], EG), v3(el[:, t, :], EG), spread(goh[:, t, :], EPG), ALU.add)
            link(op)
            link(V.tensor_reduce(R(4), em, AX.X, ALU.max))

            def first_of(oh, vals, top, cand):
                link(TT(oh, vals, spread(top, NE), ALU.is_equal))
                link(TT(oh, oh, spread_mid(ir32, NT), ALU.mult))
                link(V.tensor_reduce(cand, oh, AX.X, ALU.max))
                link(TT(oh, oh, spread(cand, NE), ALU.is_equal))

            first_of(oh1, em, R(4), R(5))
            link(STT(em2, oh1, -3.0 * BIG, em, ALU.mult, ALU.add))
            link(V.tensor_reduce(R(6), em2, AX.X, ALU.max))
            TT(R(8), R(6), R(4), ALU.subtract).then_inc(r_lt, 1)
            first_of(oh2, em2, R(6), R(7))
            link(TT(Msel, oh1, oh2, ALU.add))
            V.tensor_copy(tokid16[:, 0:NT], tokid).then_inc(r_step, 1)
            dve.wait_ge(r_exp, 2)
            link(TS(R(9), R(8), 1.0, None, ALU.add))
            link(V.reciprocal(R(9), R(9)))
            link(TT(R(10), R(2), R(9), ALU.mult))
            link(V.tensor_copy(eweight[:, 0, :], R(10)))
            link(TT(eweight[:, 1, :], R(10), R(8), ALU.mult))
            dve.wait_ge(rank_mm, 1)
            link(V.tensor_copy(rankm, v3(banks[5][:, 0:NT * NE], NT)))
            link(V.tensor_reduce(rrow[:, 0:1], banks[6][:, 0:NE], AX.X, ALU.max))
            link(TS(rrow[:, 8:8 + PASSES], iota64[:, 0:PASSES], float(SLOTS), None, ALU.mult))
            link(TT(rrow[:, 8:8 + PASSES], rrow[:, 0:1].broadcast_to([128, PASSES]), rrow[:, 8:8 + PASSES], ALU.is_gt))
            link(V.tensor_reduce(rrow[:, 1:2], rrow[:, 8:8 + PASSES], AX.X, ALU.add))
            for k, oh in enumerate((oh1, oh2)):
                link(TT(c1, oh, spread_mid(ie32, NT), ALU.mult))
                link(V.tensor_reduce(R(12 + 2 * k), c1, AX.X, ALU.add))
                link(TT(c1, oh, rankm, ALU.mult))
                link(V.tensor_reduce(R(13 + 2 * k), c1, AX.X, ALU.add))
                link(TS(R(12 + 2 * k), R(12 + 2 * k), float(SLOTS), None, ALU.mult))
            link(STT(rankm, Msel, 1000.0, rankm, ALU.mult, ALU.add))
            link(TS(rankm, rankm, 1000.0, None, ALU.subtract))
            link(V.memset(idx_all, 0))
            V.tensor_copy(npass_i[:, 0:1], rrow[:, 1:2]).then_inc(pass_ready, 1)
            dve.wait_ge(pass_ready, 1)

            n_pass = dve.value_load(npass_i[0:1, 0:1], min_val=1, max_val=PASSES)
            dve.sem_inc(xe_evac, 2)
            mlink = Chain(dve, mch)
            with dve.Fori(0, n_pass) as p:
                mlink.loop(p, 14)
                for t in range(NT):
                    last = TT(pick[:, t, :].rearrange("p (e s) -> p e s", s=SLOTS), spread(rankm[:, t, :], SLOTS),
                              spread_mid(iota64, NE), ALU.is_equal)
                last.then_inc(pick_ready, 1)
                dve.wait_ge(pick_ready, p + 1)
                mlink(TS(rankm, rankm, float(SLOTS), None, ALU.subtract))
                for k in range(2):
                    expert, rank = R(12 + 2 * k), R(13 + 2 * k)
                    mlink(TS(R(17), rank, float(SLOTS), None, ALU.is_lt))
                    mlink(STT(R(17), rank, 0.0, R(17), ALU.is_ge, ALU.mult))
                    mlink(TT(R(18), expert, rank, ALU.add))
                    mlink(TT(R(18), R(18), R(17), ALU.mult))
                    V.tensor_copy(ridx[:, k * NT:(k + 1) * NT], R(18))
                    mlink(TT(pweight[:, k, :], eweight[:, k, :], R(17), ALU.mult))
                    mlink(TS(rank, rank, float(SLOTS), None, ALU.subtract))
                dve.wait_ge(idx_mm, p * PAIRS + PAIRS)
                mlink(V.tensor_copy(idx_all[:, 0:PAIRS], banks[0][:, 0:PAIRS]))

                def next_indices(q):
                    V.tensor_copy(idx_cur, idx_all[:, ds(q, 1)] if not isinstance(q, int) else idx_all[:, q:q + 1]).then_inc(idx_ready, 1)

                def next_tokens(n):
                    for b in range(4):
                        dve.wait_ge(xe_tr, n * 4 + b + 2)
                        TT(xe[:, 4 * b:4 * b + 4, :], v3(banks[4 + b % 2][:, :], 4),
                           spread(pcol[:, P_GFFN + 4 * b:P_GFFN + 4 * b + 4], 128), ALU.mult).then_inc(xe_evac, 1)

                next_indices(0)
                next_tokens(p * (PAIRS + 1))
                with dve.Fori(0, PAIRS) as q:
                    next_indices(q + 1)
                    for x in range(2):
                        E = p * NE + 2 * q + x
                        dve.wait_ge(e_step, 8 * E + 8 + 4)
                        dve.wait_ge(gu_act, E + 2)
                        dve.wait_ge(e_step, 8 * E + 8)
                        TT(hid[x], hsil[x], v3(banks[2 * x + 1][:, 0:256], FC), ALU.mult).then_inc(gu_done, 1)
                    next_tokens(p * (PAIRS + 1) + q + 1)
                for n in range(2 * NT):
                    k, t = n % 2, n // 2
                    dve.wait_ge(comb_in[n % 2], p * (16 * NT) + 16 * (n // 2 + 1))
                    STT(x_res[:, t, :], cg[n % 2], pweight[:, k, t:t + 1], x_res[:, t, :], ALU.mult, ALU.add).then_inc(comb_done, 1)
                    dve.wait_ge(comb_done, p * (2 * NT) + n + 2)
                mlink.end(1, 14)

            for t in range(NT):
                norm_tile(2 * NT + t, x_res[:, t, :], P_GPLE, xn2T, t)
            with dve.Fori(0, 4) as i:
                for n in range(6):
                    dve.wait_ge(ple_sig, 6 * i + n + 1)
                    xr = x_res[:, n % 3, ds(i * 512 + (n // 3) * SLAB, SLAB)]
                    TT(gsig[n % 2], gsig[n % 2], banks[n][:, SLAB:2 * SLAB], ALU.mult).then_inc(ple_step, 1)
                    dve.wait_ge(ple_step, 6 * i + n + 1)
                    TT(xr, xr, gsig[n % 2], ALU.add).then_inc(ple_done, 1)
            for t in range(NT):
                dve.wait_ge(f_sq, t + 1)
                TS(sm[:, 4 + t:5 + t], sm[:, t:t + 1], 1.0 / D, EPS, ALU.mult, ALU.add).then_inc(f_ms, 1)
                dve.wait_ge(f_rt, t + 1)
                V.reciprocal(sm[:, 12 + t:13 + t], sm[:, 8 + t:9 + t]).then_inc(f_rc, 1)
                dve.wait_ge(f_rc, t + 1)
                STT(yfin[t % 2], x_res[:, t, :], sm[:, 12 + t:13 + t], gfin, ALU.mult, ALU.mult).then_inc(f_ok, 1)

        @block.tensor
        def _(pe):
            mm, tr = nc.tensor.matmul, nc.tensor.transpose
            pe.sem_inc(proj_done, 2)
            for started in (y_mm, l_mm, xe_tr):
                pe.sem_inc(started, 1)
            pe.sem_inc(mix_mm, 2)
            pe.sem_inc(wo_mm, 3)
            pe.sem_inc(ple_mm, 3)
            pe.sem_inc(e_step, 8)
            pe.wait_ge(consts_ready, CONSTS)
            pe.wait_ge(params_in, 16 * PARAM_DMAS)
            for b in range(3):
                last = tr(banks[6][:, 128 * b:128 * b + 128], prow[:, b, :], ident)
            last.then_inc(ptr_done, 1)
            pe.wait_ge(setup_in, 16 * 7)
            for b in range(2):
                for c in range(20):
                    last = tr(banks[4 + b][:, 24 * c:24 * c + 24], hist_rows[:, (20 * b + c) * 128:(20 * b + c + 1) * 128], ident[0:24, 0:24])
                last.then_inc(hist_T, 1)
            tr(banks[7][:, 0:128], sm[:, 0:128], ident).then_inc(hist_T, 1)

            def norm_T(n):
                pe.wait_ge(n_scaled, n + 1)
                for b in range(4):
                    pe.wait_ge(n_evac, 4 * n + b + 1)
                    for q in range(4):
                        last = tr(banks[b][:, 128 * q:128 * q + 128], nrm[n % 2][:, (4 * b + q) * 128:(4 * b + q + 1) * 128], ident)
                    last.then_inc(n_tr, 1)

            for t in range(NT):
                norm_T(t)
            pe.wait_ge(n_evac, 12 + 4)
            pe.wait_ge(dt_loaded, 16)
            pe.wait_ge(hist_evac, 3)
            for k in range(KC):
                last = mm(banks[4][0:HEADS, 0:T], w_dt[:, k, :], xnT[:, k, :], start=(k == 0), stop=(k == KC - 1))
            last.then_inc(dt_done, 1)

            def dt_columns():
                pe.wait_ge(dt_step, 5)
                for n, (src, t) in enumerate([(dtT, 0), (dtT, 1), (dtT, 2), (cumT, 0), (cumT, 1), (cumT, 2),
                                              (ddT, 0), (ddT, 1), (ddT, 2), (ddfT, 0)]):
                    last = tr(banks[5][:, 32 * n:32 * n + 32], src[:, t * 128:(t + 1) * 128], ident[0:32, 0:32])
                last.then_inc(dt_tr, 1)
            dt_columns()

            with pe.Fori(0, GROUPS) as g:
                def group_slab(m, w):
                    for c in range(2):
                        pe.wait_ge(proj_free, 10 * g + m + c + 1)
                        for k in range(KC):
                            last = mm(banks[(m + c) % 2][:, 0:T], w[:, k, c * 128:(c + 1) * 128], xnT[:, k, :],
                                      start=(k == 0), stop=(k == KC - 1))
                        last.then_inc(proj_done, 1)
                pe.wait_ge(side_loaded, 32 * g + 32)
                group_slab(0, slab[2])
                pe.wait_ge(slab_loaded[0], 32 * g + 16)
                group_slab(2, slab[0])
                pe.wait_ge(slab_loaded[1], 32 * g + 16)
                group_slab(4, slab[1])
                pe.wait_ge(slab_loaded[0], 32 * g + 32)
                group_slab(6, slab[0])
                pe.wait_ge(silu_done, 6 * g + 6 + 2)
                pe.wait_ge(y_free, 4 * g + 1)
                pe.wait_ge(hn_done, 4 * g + 1)
                for t in range(NT):
                    last = mm(banks[2][:, t * 128:(t + 1) * 128], BT[:, t * 128:(t + 1) * 128], CT[:, t * 128:(t + 1) * 128],
                              start=True, stop=True)
                last.then_inc(aux_done, 1)
                for t in range(NT):
                    last = tr(banks[3][:, t * 128:(t + 1) * 128], BT[:, t * 128:(t + 1) * 128], ident)
                last.then_inc(aux_done, 1)
                for t in range(NT):
                    for j in range(4):
                        last = tr(banks[4 + t][:, j * 128:(j + 1) * 128], xsT[:, j, t * 128:(t + 1) * 128], ident)
                    last.then_inc(aux_done, 1)
                pe.wait_ge(slab_loaded[1], 32 * g + 32)
                group_slab(8, slab[1])
                pe.wait_ge(aux_evac, 3 * g + 3)
                mm(banks[7][:, :], Btok[:, 0, :], x_dd[:, 0, :], start=True, stop=True).then_inc(hT0_done, 1)
                for j in range(4):
                    mm(banks[3][:, j * 128:(j + 1) * 128], x_ddf[:, j * 128:(j + 1) * 128], Btok[:, 0, :], start=True, stop=False)
                    last = mm(banks[3][:, j * 128:(j + 1) * 128], x_dd[:, 1, j * 128:(j + 1) * 128], Btok[:, 1, :], start=False, stop=True)
                last.then_inc(pst_done, 1)
                pe.wait_ge(w_ready, g + 1)
                pe.wait_ge(hT0_evac, g + 1)
                pe.wait_ge(pst_evac, g + 1)
                for j in range(4):
                    pe.wait_ge(h0_loaded[j % 2], 32 * g + 16 * (j // 2 + 1))
                    for b in range(NSEQ):
                        last = tr(banks[2 + b // 4][:, (b % 4) * 128:(b % 4 + 1) * 128], h0[j % 2][:, b, :], ident)
                    last.then_inc(h0_tr, 1)
                    pe.wait_ge(y_free, 4 * g + j + 1)
                    for t in range(NT):
                        for h in range(2):
                            mm(banks[5][h * 64:h * 64 + 64, t * 128:(t + 1) * 128],
                               x_dt[:, t, j * 128 + h * 64:j * 128 + h * 64 + 64],
                               decay[:, 2 * j + h, t * 128:(t + 1) * 128], start=True, stop=True)
                    mm(banks[4][:, 128:256], hT0[:, j * 128:(j + 1) * 128], CT[:, 128:256], start=True, stop=True)
                    pe.wait_ge(h0T_evac, 4 * g + j + 1)
                    for b in range(NSEQ):
                        s = slice(SEQ + b * SLEN, SEQ + (b + 1) * SLEN)
                        last = mm(banks[4][:, s], h0T[:, b, :], CT[:, s], start=True, stop=True)
                    last.then_inc(y_mm, 1)
                    pe.wait_ge(hn_done, 4 * g + j + 1)
                    for half in range(2):
                        last = mm(banks[6 + half][:, :], x_dd[:, 2, j * 128:(j + 1) * 128], Bseg[:, 4 * half:4 * half + 4, :],
                                  start=True, stop=True)
                    last.then_inc(st_mm, 1)

            with pe.Fori(0, GROUPS) as g:
                for s in range(4):
                    pe.wait_ge(slab_loaded[s % 2], 32 * g + (s // 2) * 16 + 128 + 16)
                    for c in range(2):
                        m = 2 * s + c
                        pe.wait_ge(proj_free, 8 * g + m + 41)
                        for k in range(KC):
                            last = mm(banks[m % 2][:, 0:T], slab[s % 2][:, k, c * 128:(c + 1) * 128], xnT[:, k, :],
                                      start=(k == 0), stop=(k == KC - 1))
                        last.then_inc(proj_done, 1)
                pe.wait_ge(side_loaded, 32 * g + 128 + 32)
                pe.wait_ge(conv_done, 4 * g + 24 + 4 + 2)
                pe.wait_ge(h0T_evac, KC)
                pe.wait_ge(hn_done, KC + 1)
                for m in range(4):
                    pe.wait_ge(l_sig, 4 * g + m + 1)
                    b = 2 + 2 * (m % 2)
                    mm(banks[b][:, 0:T], lw[:, m, :], xl[:, m, :], start=True, stop=True)
                    mm(banks[b + 1][:, 0:T], lw[:, 4 + m, :], xl[:, m, :], start=True, stop=True).then_inc(l_mm, 1)

            pe.wait_ge(l_done, GROUPS + 1)
            for q in range(10):
                if q >= 2:
                    pe.wait_ge(tails_evac, q - 1)
                for r in range(4):
                    last = tr(banks[6 + q % 2][0:27, r * 128:(r + 1) * 128], convmem[:, 4 * q + r, :], ident)
                last.then_inc(tails_T, 1)
            pe.wait_ge(tails_evac, 9)
            tr(banks[6][0:16, 0:128], lru_end[:, 0, :], ident)
            tr(banks[6][:, 128:256], lru_end[:, 1:9, :], ident).then_inc(tails_T, 1)
            pe.wait_ge(l_sig, KC + 2)
            mm(banks[5][:, 0:T], ones, ss_acc, start=True, stop=True).then_inc(rs_mm, 1)
            pe.wait_ge(rs_ms, 1)
            pe.wait_ge(tails_evac, 12)
            pe.wait_ge(proj_free, 72 + 2)

            with pe.Fori(0, 8) as i:
                for s, rhs in enumerate((xnT, Y, xnT, H)):
                    pe.wait_ge(slab_loaded[s % 2], 32 * i + (s // 2) * 16 + 256 + 16)
                    for cc in range(2):
                        pe.wait_ge(mix_done, 2 * i + cc + 1)
                        for k in range(KC):
                            last = mm(banks[2 * s + cc][:, 0:T], slab[s % 2][:, k, cc * 128:(cc + 1) * 128], rhs[:, k, :],
                                      start=(k == 0), stop=(k == KC - 1))
                        last.then_inc(mix_mm, 1)
            pe.wait_ge(mix_done, KC + 2)
            with pe.Fori(0, 4) as i:
                for s in range(2):
                    pe.wait_ge(slab_loaded[s], 16 * i + 512 + 16)
                    for t in range(NT):
                        pe.wait_ge(wo_done, 6 * i + 3 * s + t + 1)
                        for k in range(KC):
                            last = mm(banks[3 * s + t][:, 0:SLAB], mixed[:, k, t * 128:(t + 1) * 128], slab[s][:, k, :],
                                      start=(k == 0), stop=(k == KC - 1))
                        last.then_inc(wo_mm, 1)
            for t in range(NT):
                norm_T(NT + t)
            pe.wait_ge(n_evac, 24 + 4)
            pe.wait_ge(router_in, 64)
            for t in range(NT):
                for k in range(KC):
                    last = mm(banks[4][:, t * 36:t * 36 + 36], xn2T[:, k, t * 128:(t + 1) * 128], w_r[:, k, :],
                              start=(k == 0), stop=(k == KC - 1))
            last.then_inc(r_mm, 1)
            pe.wait_ge(r_step, 1)
            for t in range(NT):
                for s in range(t + 1):
                    mm(banks[5][:, t * NE:(t + 1) * NE], before if s == t else ones, Msel[:, s, :], start=(s == 0), stop=(s == t))
            for t in range(NT):
                last = mm(banks[6][:, 0:NE], ones, Msel[:, t, :], start=(t == 0), stop=(t == NT - 1))
            last.then_inc(rank_mm, 1)

            pe.wait_ge(pass_ready, 1)
            n_pass = pe.value_load(npass_i[0:1, 0:1], min_val=1, max_val=PASSES)
            with pe.Fori(0, n_pass) as p:
                pe.wait_ge(pick_ready, p + 1)
                pe.wait_ge(gu_act, p * NE + 1)
                pe.sem_inc(wait_stop, 1)
                with pe.Fori(0, PAIRS) as q:
                    for t in range(NT):
                        last = mm(banks[0][:, ds(q, 1)], pick[:, t, ds(q * 128, 128)], tokid16[:, t:t + 1], start=(t == 0), stop=(t == NT - 1))
                    last.then_inc(idx_mm, 1)

                def tokens_T(n):
                    pe.wait_ge(gathered, n * 16 + 16)
                    for b in range(4):
                        pe.wait_ge(xe_evac, n * 4 + b + 1)
                        for q4 in range(4):
                            last = tr(banks[4 + b % 2][:, q4 * 128:(q4 + 1) * 128], xg[:, (4 * b + q4) * 128:(4 * b + q4 + 1) * 128], ident)
                        last.then_inc(xe_tr, 1)

                tokens_T(p * (PAIRS + 1))
                with pe.Fori(0, PAIRS) as q:
                    for x in range(2):
                        E = p * NE + 2 * q + x
                        pe.wait_ge(xe_evac, (p * (PAIRS + 1) + q) * 4 + 4 + 2)
                        pe.wait_ge(gu_done, E + 1)
                        for s in range(4):
                            pe.wait_ge(ew_loaded[s], 16 * E + 16)
                            half, w8 = s % 2, v3(slot[s], KC // 2)
                            for f in range(FC):
                                for k in range(KC // 2):
                                    last = mm(banks[2 * x + s // 2][:, f * SLOTS:(f + 1) * SLOTS], w8[:, k, f * 128:(f + 1) * 128],
                                              xe[:, 8 * half + k, x * SLOTS:(x + 1) * SLOTS], start=(half == 0 and f == 0 and k == 0),
                                              stop=(half == 1 and k == KC // 2 - 1), skip_group_check=True)
                            last.then_inc(e_step, 1)
                        if x == 1:
                            tokens_T(p * (PAIRS + 1) + q + 1)
                        pe.wait_ge(gu_done, E + 2)
                        for b in range(4):
                            if b % 2 == 0:
                                pe.wait_ge(ew_loaded[4 + b // 2], 16 * E + 16)
                            pe.wait_ge(dn_free, 4 * E + b + 1)
                            wd = v3(slot[4 + b // 2], FC)
                            for f in range(FC):
                                last = mm(banks[6 + b % 2][0:SLOTS, :], hid[x][:, f, :], wd[:, f, (b % 2) * 512:(b % 2) * 512 + 512],
                                          start=(f == 0), stop=(f == FC - 1))
                            last.then_inc(e_step, 1)

            for t in range(NT):
                norm_T(2 * NT + t)
            pe.wait_ge(p_loaded, 16 * NT)
            for h in range(2):
                for t in range(NT):
                    last = tr(banks[4 + h][:, t * 128:(t + 1) * 128], p_in[:, t, h * 128:(h + 1) * 128], ident)
            last.then_inc(p_T, 1)
            pe.wait_ge(p_evac, 2)
            pe.wait_ge(n_evac, 36 + 4)
            pe.wait_ge(ple_in, 16)
            with pe.Fori(0, 4) as i:
                for s in range(2):
                    pe.wait_ge(pslab[s], 16 * i + 16)
                    for t in range(NT):
                        pe.wait_ge(ple_done, 6 * i + 3 * s + t + 1)
                        bank = banks[3 * s + t]
                        for k in range(KC):
                            mm(bank[:, 0:SLAB], xn2T[:, k, t * 128:(t + 1) * 128], slab[s][:, k, :], start=(k == 0), stop=(k == KC - 1))
                        for k in range(2):
                            last = mm(bank[:, SLAB:2 * SLAB], pT[:, k, t * 128:(t + 1) * 128], w_ple_sb[:, k, ds(i * 512 + s * SLAB, SLAB)],
                                      start=(k == 0), stop=(k == 1))
                        last.then_inc(ple_mm, 1)


_INS = ['x_prompt', 'x_sample', 'state_ssm', 'state_ssm_conv', 'state_lru', 'state_lru_conv', 'p_prompt', 'p_sample',
        'g_mix', 'w_in', 'conv_m_w', 'conv_m_b', 'dt_bias', 'a_log', 'd_skip', 'g_ssm', 'w_out_m',
        'conv_r_w', 'conv_r_b', 'w_lru_a', 'b_lru_a', 'w_lru_x', 'b_lru_x', 'lru_lambda', 'w_out_r', 'w_o',
        'g_ffn', 'w_router_group', 'b_router_group', 'w_router_expert', 'b_router_expert',
        'w_exp_gate', 'w_exp_up', 'w_exp_down', 'g_ple', 'w_ple_gate', 'w_ple', 'g_final']
_OUTS = [(1, SEQ, D), (NSEQ, SLEN, D),
         (1, 1, HEADS, HP, NST), (1, 1, HIST, XBC), (1, 1, D), (1, 1, HIST, D),
         (1, NSEQ, HEADS, HP, NST), (1, NSEQ, HIST, XBC), (1, NSEQ, D), (1, NSEQ, HIST, D)]


def kernel(**inputs):
    import numpy as _np
    import concourse.bacc as _bacc
    from concourse import mybir as _mybir
    from concourse.bass_utils import run_bass_kernel_spmd as _run

    nc = _bacc.Bacc("TRN2", target_bir_lowering=False, num_devices=1)
    arrays, ins = {}, {}
    f32 = _mybir.dt.float32
    for name in _INS:
        x = _np.ascontiguousarray(inputs[name])
        arrays[f"in_{name}_dram"] = x
        ins[name] = nc.dram_tensor(f"in_{name}_dram", x.shape, _mybir.dt.from_np(x.dtype), kind="ExternalInput").ap()
    outs = [nc.dram_tensor(f"out_{i}_dram", s, f32, kind="ExternalOutput").ap() for i, s in enumerate(_OUTS)]
    scratch = [nc.dram_tensor(n, s, f32).ap() for n, s in
               (("cumulated_decays", (HEADS, T)), ("normalised_rows", (T, D)), ("expert_rows", (NE * SLOTS, D)))]
    hybrid_stream_step(nc, ins, outs, scratch)
    r = _run(nc, [arrays], core_ids=[0])
    return tuple(r.results[0][f"out_{i}_dram"] for i in range(len(_OUTS)))
```

```python
import concourse.bass as bass
from concourse import mybir
from contextlib import ExitStack

PARAM_DMAS, CONSTS = 13, 14
SSD_LINKS, LRU_LINKS = 50, 24

D = 2048
KC = D // 128
SEQ, NSEQ, SLEN = 256, 8, 16
T = SEQ + NSEQ * SLEN
NT = T // 128
HEADS, HP, NST, GROUPS = 32, 64, 128, 4
HPG = HEADS // GROUPS
XBC = D + 2 * GROUPS * NST
TAPS = 4
HIST = TAPS - 1
PADDED = HIST + SEQ + NSEQ * (HIST + SLEN)
CONV = PADDED - HIST
S0 = SEQ + HIST
SPAD = SLEN + HIST
OFF_Z, OFF_X = 0, D
OFF_B, OFF_C = OFF_X + D, OFF_X + D + GROUPS * NST
OFF_DT = OFF_X + XBC
OFF_GY = OFF_DT + HEADS
OFF_XL = OFF_GY + D
OFF_GM = OFF_XL + D
OFF_GR = OFF_GM + D
EG, EPG = 4, 8
NE = EG * EPG
FF = D // 4
FC = FF // 128
SLOTS = 64
PASSES = T // SLOTS
PAIRS = NE // 2
PLE = 256
EPS = 1e-6
SLAB = 256
SLABF = KC * SLAB
BIG = 1.0e30

P_GMIX, P_GFFN, P_GPLE, P_GSSM = 0, 16, 32, 48
P_BA, P_BX, P_LAM, P_CB = 64, 80, 96, 112
P_CW = 152
P_CR = P_CW + TAPS * 24
P_ROWS = P_CR + TAPS * 16
NCONV = 40

C_DT, C_CUM, C_DD, C_DDF = 0, 3, 6, 9


def hybrid_stream_step(nc, a, outs, scr):
    fp32, i32 = mybir.dt.float32, mybir.dt.int32
    ALU, ACT, AX = mybir.AluOpType, mybir.ActivationFunctionType, mybir.AxisListType
    ds = bass.ds
    (y_p, y_s, ssm_p, sconv_p, lru_p, lconv_p, ssm_s, sconv_s, lru_s, lconv_s) = outs
    acum_d, y_d = scr

    ctx = ExitStack()
    with ctx:
        arena = ctx.enter_context(nc.sbuf_tensor("arena", [128, 53200], fp32))
        banks = [ctx.enter_context(nc.psum_tensor(f"bank{i}", [128, 512], fp32)) for i in range(8)]

        def sem(name):
            return ctx.enter_context(nc.semaphore(name))

        class Region:
            def __init__(self, start, size):
                self.at, self.end = start, start + size

            def take(self, n, parts=128):
                self.at += n
                assert self.at <= self.end, (self.at, self.end)
                return arena[0:parts, self.at - n:self.at]

        def v3(ap, x):
            return ap.rearrange("p (x y) -> p x y", x=x)

        RING, RA, RY, RH, RT = 0, 6 * SLABF, 6 * SLABF + 6144, 6 * SLABF + 2 * 6144, 6 * SLABF + 3 * 6144
        slot = [arena[:, s * SLABF:(s + 1) * SLABF] for s in range(6)]
        slab = [v3(s, KC) for s in slot]
        xnT = v3(arena[:, RA:RA + 6144], KC)
        x_res = v3(arena[:, RA:RA + 6144], NT)
        Y = v3(arena[:, RY:RY + 6144], KC)
        H = v3(arena[:, RH:RH + 6144], KC)
        x_in = v3(arena[:, RH:RH + 6144], NT)
        hist_rows = arena[0:NSEQ * HIST, RY:RY + XBC + D]

        keep = Region(RT, 4040)
        ident = keep.take(128)
        ones = keep.take(128)
        before = keep.take(128)
        causal = v3(keep.take(256), 2)
        stream_of = keep.take(NSEQ)
        pcol = keep.take(384)
        convmem = v3(keep.take(NCONV * 27), NCONV)
        tokcol = v3(keep.take(10 * HEADS), 10)
        lru_h0 = v3(keep.take(128), NSEQ)
        lru_end = v3(keep.take(16 * 9), 9)
        ss_acc = keep.take(T)
        rstdB = keep.take(T)
        dskip = keep.take(KC)
        lam_c = keep.take(KC)
        sm = keep.take(256)
        iota64 = keep.take(64)
        rtail = Region(keep.at, RT + 10192 - keep.at)
        mixed = v3(rtail.take(6144), KC)
        under = Region(RT + keep.at - RT, 6144)
        raw = [under.take(PADDED) for _ in range(2)]
        acc = [under.take(PADDED) for _ in range(2)]

        rs = Region(3 * SLABF, 3 * SLABF)
        decay = v3(rs.take(HPG * T), HPG)
        growth = v3(rs.take(4 * T), 4)
        xsT = v3(rs.take(4 * T), 4)
        x_dt = v3(rs.take(NT * 512), NT)
        x_dd = v3(rs.take(NT * 512), NT)
        h0 = [v3(rs.take(NSEQ * NST), NSEQ) for _ in range(2)]
        x_ddf = rs.take(512)
        hT0 = rs.take(512)
        rh = Region(RH, 6144)
        h0T = v3(rh.take(NSEQ * 128), NSEQ)
        Bseg = v3(rh.take(NSEQ * NST), NSEQ)
        BT, CT = rh.take(T), rh.take(T)
        Btok = v3(rh.take(NT * NST), NT)
        cbm = v3(rh.take(NT * 128), NT)
        pst = v3(rh.take(512), 4)
        ytmp = [rh.take(T) for _ in range(2)]
        ysq = [rh.take(T) for _ in range(2)]
        dec = rh.take(NSEQ)

        rl = Region(3 * SLABF, 3 * SLABF)
        xl, gy, lr, li, la_, lt = (v3(rl.take(4 * T), 4) for _ in range(6))
        lw = v3(slot[2][:, 0:1024], 8)

        rm = Region(3 * SLABF, SLABF)
        sg_m, sg_r, t_m, t_r = ([rm.take(T) for _ in range(2)] for _ in range(4))

        rd = Region(3 * SLABF, SLABF)
        dtT, dA, cumT, ddT, dtmp, dtmp2, rmask = (rd.take(T, 32) for _ in range(7))
        ddfT = rd.take(128, 32)
        dcol = rd.take(8, 32)
        w_dt = v3(slot[5][:, 512:512 + KC * HEADS], KC)
        nrm = [slot[4][:, 0:D], slot[4][:, D:2 * D]]
        prow = v3(slot[5][:, 0:384], 3)
        consts_ready = sem("consts_ready")
        params_in = sem("params_in")
        setup_in = sem("setup_in")
        x_loaded = [sem(f"x_loaded{t}") for t in range(NT)]
        ptr_done = sem("ptr_done")
        hist_T, hist_evac = sem("hist_T"), sem("hist_evac")
        n_sq, n_ms, n_rt, n_scaled = sem("n_sq"), sem("n_ms"), sem("n_rt"), sem("n_scaled")
        n_tr, n_evac = sem("n_tr"), sem("n_evac")
        dt_loaded, dt_done, dt_step, dt_act = sem("dt_loaded"), sem("dt_done"), sem("dt_step"), sem("dt_act")
        dt_tr, cum_stored = sem("dt_tr"), sem("cum_stored")
        slab_loaded = [sem("slab_loaded0"), sem("slab_loaded1")]
        side_loaded = sem("side_loaded")
        proj_done, proj_free = sem("proj_done"), sem("proj_free")
        conv_done, silu_done = sem("conv_done"), sem("silu_done")
        cum_loaded, seg_ready, exp_done = sem("cum_loaded"), sem("seg_ready"), sem("exp_done")
        aux_done, aux_evac, w_ready = sem("aux_done"), sem("aux_evac"), sem("w_ready")
        hT0_done, hT0_evac = sem("hT0_done"), sem("hT0_evac")
        pst_done, pst_evac, pst_stored = sem("pst_done"), sem("pst_evac"), sem("pst_stored")
        h0_loaded, h0_tr, h0T_evac = [sem("h0_loaded0"), sem("h0_loaded1")], sem("h0_tr"), sem("h0T_evac")
        y_mm, y_free, y_done, y_act = sem("y_mm"), sem("y_free"), sem("y_done"), sem("y_act")
        st_mm, hn_done, hn_stored = sem("st_mm"), sem("hn_done"), sem("hn_stored")
        dch = sem("dch")
        l_mm, l_sig, l_la, l_at, l_w, l_s, l_done = (sem("l_mm"), sem("l_sig"), sem("l_la"), sem("l_at"),
                                                     sem("l_w"), sem("l_s"), sem("l_done"))
        rs_mm, rs_ms, rs_rt = sem("rs_mm"), sem("rs_ms"), sem("rs_rt")
        mix_mm, mix_sig, mix_done = sem("mix_mm"), sem("mix_sig"), sem("mix_done")
        x_again, wo_mm, wo_done = sem("x_again"), sem("wo_mm"), sem("wo_done")
        tails_T, tails_evac, tails_stored = sem("tails_T"), sem("tails_evac"), sem("tails_stored")

        xn2T = Y
        rr = Region(RH + 2816, 2560)
        w_r = v3(rr.take(KC * 36), KC)
        rbias = rr.take(36)
        L = v3(rr.take(NT * 36), NT)
        em, c1, oh1, oh2, Msel, rankm, em2 = (v3(rr.take(NT * NE), NT) for _ in range(7))
        goh = v3(rr.take(NT * EG), NT)
        ge = v3(rr.take(NT * EG), NT)
        ie32 = rr.take(NE)
        ir32 = rr.take(NE)
        rcol = v3(rr.take(24 * NT), 24)
        rrow = rr.take(16)
        npass_i = rr.take(2).bitcast(i32)
        ridx = rr.take(2 * NT).bitcast(i32)
        eweight = v3(rr.take(2 * NT), 2)
        pweight = v3(rr.take(2 * NT), 2)
        rx = Region(RY, 6144)
        xe = v3(rx.take(KC * 128), KC)
        yrow = v3(rx.take(2 * 512), 2)
        rq = Region(keep.at, 6144)
        xtok = [rq.take(D), rq.take(D), arena[:, RH + 2 * T:RH + 2 * T + D]]
        pick = v3(rq.take(NT * 128), NT)
        hid = [v3(rq.take(FC * SLOTS), FC) for _ in range(2)]
        hrow = [rq.take(FF // 2) for _ in range(2)]
        pT = v3(arena[:, RH:RH + 2 * T], 2)
        p_in = v3(arena[:, RH + 5376:RH + 5376 + NT * PLE], NT)
        assert NT * PLE == 768
        w_ple_sb = v3(slot[2], 2)
        gsig = [arena[:, RH + 2048 + 256 * i:RH + 2304 + 256 * i] for i in range(2)]
        gfin = slot[3][:, 0:D]
        yfin = [slot[3][:, D:2 * D], slot[4][:, 0:D], slot[4][:, D:2 * D]]
        cg = [slot[i][:, h * D:(h + 1) * D] for i in (0, 1, 5) for h in range(2)]

        router_in, r_mm, r_lt, r_exp, r_step = sem("router_in"), sem("r_mm"), sem("r_lt"), sem("r_exp"), sem("r_step")
        rank_mm, pass_ready = sem("rank_mm"), sem("pass_ready")
        pick_ready = sem("pick_ready")
        xe_tr, xe_evac = sem("xe_tr"), sem("xe_evac")
        ew_loaded = [sem("gate_loaded"), sem("up_loaded"), sem("down_loaded")]
        e_step = sem("e_step")
        gu_act, h_mul, h_tr, gu_done = sem("gu_act"), sem("h_mul"), sem("h_tr"), sem("gu_done")
        yrow_out = [sem("yrow_out0"), sem("yrow_out1")]
        mch, dn_free, p_loaded, ple_step, f_rc = sem("mch"), sem("dn_free"), sem("p_loaded"), sem("ple_step"), sem("f_rc")
        comb_in, comb_done = [sem(f"comb_in{n}") for n in range(2 * NT)], sem("comb_done")
        ple_in, p_T, p_evac = sem("ple_in"), sem("p_T"), sem("p_evac")
        ple_mm, ple_sig, ple_done = sem("ple_mm"), sem("ple_sig"), sem("ple_done")
        pslab = [sem("pslab0"), sem("pslab1")]
        f_sq, f_ms, f_rt, f_ok = sem("f_sq"), sem("f_ms"), sem("f_rt"), sem("f_ok")
        f_out = [sem(f"f_out{t}") for t in range(NT)]
        gfin_in = sem("gfin_in")

        w_in = a["w_in"]

        def staging(n):
            return xtok[n - NT] if NT <= n < 2 * NT else nrm[n % 2]

        def cols(w, at):
            return w[0, :, ds(at, SLAB)].rearrange("(k p) c -> p k c", p=128)

        class Chain:
            def __init__(self, eng, s):
                self.eng, self.s, self.base, self.k = eng, s, 0, 0

            def __call__(self, ins):
                self.k += 1
                ins.then_inc(self.s, 1)
                self.eng.wait_ge(self.s, self.base + self.k)

            def loop(self, i, per):
                self.start = self.base + self.k
                self.base, self.k = self.start + i * per, 0

            def end(self, trips, per):
                assert self.k == per, self.k
                self.base, self.k = self.start + trips * per, 0

        def ridx_col(k, t):
            return ridx[:, k * NT + t:k * NT + t + 1]

        def spread(ap, n):
            return ap.unsqueeze(len(ap.shape)).broadcast_to(list(ap.shape) + [n])

        def spread_mid(ap, n):
            return ap.unsqueeze(1).broadcast_to([ap.shape[0], n] + list(ap.shape[1:]))

        def streams(ap):
            return ap[:, SEQ:T].rearrange("p (b t) -> p b t", t=SLEN)

        def pstreams(ap):
            return ap[:, S0:PADDED].rearrange("p (b t) -> p b t", t=SPAD)

        lru_rows = slot[5][:, 1536:1664]
        tail_rows = arena[0:27, 4 * SLABF:4 * SLABF + NCONV * 128]
        ss_c, ms_c, rt_c, rstd_c = 128, 140, 152, 164
        lam_s = 176

        wait_stop = sem("wait_stop")

        block = ctx.enter_context(nc.Block())

        @block.sync
        def _(sp):
            for t in range(NT):
                src = a["x_prompt"][0, t * 128:(t + 1) * 128, :] if t < 2 else a["x_sample"].rearrange("b s d -> (b s) d")
                sp.dma_start(x_in[:, t, :], src).then_inc(x_loaded[t], 16)
            sp.dma_start(w_dt, w_in[0, :, OFF_DT:OFF_DT + HEADS].rearrange("(k p) c -> p k c", p=128)).then_inc(dt_loaded, 16)
            sp.wait_ge(params_in, 16 * PARAM_DMAS)

            def load_slab(parity, w, at, used, count):
                sp.wait_ge(used, count)
                sp.sem_inc(wait_stop, 1)
                sp.dma_start(slab[parity], cols(w, at)).then_inc(slab_loaded[parity], 16)

            with sp.Fori(0, GROUPS) as g:
                sp.wait_ge(proj_done, 10 * g + 1)
                for n, off in enumerate((OFF_B, OFF_C)):
                    sp.dma_start(slab[2][:, :, n * 128:(n + 1) * 128],
                                 w_in[0, :, ds(g * NST + off, NST)].rearrange("(k p) c -> p k c", p=128)).then_inc(side_loaded, 16)
                load_slab(0, w_in, g * 512 + OFF_X, proj_done, 10 * g + 1)
                load_slab(1, w_in, g * 512 + OFF_X + SLAB, proj_done, 10 * g + 2)
                sp.wait_ge(cum_stored, 16)
                sp.wait_ge(dt_tr, 1)
                sp.wait_ge(y_done, 4 * g + 1)
                sp.wait_ge(y_mm, 4 * g + 1)
                sp.dma_start(decay, acum_d[ds(g * HPG, HPG), :].partition_broadcast(128)).then_inc(cum_loaded, 16)
                for half in range(2):
                    sp.dma_start(growth[half * 64:(half + 1) * 64, :, :],
                                 acum_d[ds(g * HPG, HPG), :].rearrange("(j h) t -> h j t", h=2)[half].partition_broadcast(64)
                                 ).then_inc(cum_loaded, 16)
                load_slab(0, w_in, g * 512 + OFF_Z, proj_done, 10 * g + 6)
                load_slab(1, w_in, g * 512 + OFF_Z + SLAB, proj_done, 10 * g + 8)
            with sp.Fori(0, GROUPS) as g:
                load_slab(0, w_in, g * 512 + OFF_XL, proj_done, 8 * g + 40)
                load_slab(1, w_in, g * 512 + OFF_XL + SLAB, proj_done, 8 * g + 42)
                sp.wait_ge(proj_done, 34)
                sp.wait_ge(l_mm, 4 * g + 1)
                for n, name in enumerate(("w_lru_a", "w_lru_x")):
                    sp.dma_start(lw[:, 4 * n:4 * n + 4, :], a[name][0, ds(g * 4, 4), :, :].rearrange("n k j -> k n j")).then_inc(side_loaded, 16)
                load_slab(0, w_in, g * 512 + OFF_GY, proj_done, 8 * g + 44)
                load_slab(1, w_in, g * 512 + OFF_GY + SLAB, proj_done, 8 * g + 46)
            with sp.Fori(0, 8) as i:
                sp.wait_ge(proj_done, 72)
                load_slab(0, w_in, i * SLAB + OFF_GM, mix_mm, 8 * i + 1)
                sp.wait_ge(proj_done, 74)
                load_slab(1, a["w_out_m"], i * SLAB, mix_mm, 8 * i + 2)
                load_slab(0, w_in, i * SLAB + OFF_GR, mix_mm, 8 * i + 4)
                load_slab(1, a["w_out_r"], i * SLAB, mix_mm, 8 * i + 6)
            sp.wait_ge(mix_mm, 66)
            with sp.Fori(0, 4) as i:
                load_slab(0, a["w_o"], i * 512, wo_mm, 6 * i + 1)
                load_slab(1, a["w_o"], i * 512 + SLAB, wo_mm, 6 * i + 3)

            w_gate, w_up, w_down = (v3(arena[:, 2 * i * SLABF:2 * (i + 1) * SLABF], n) for i, n in ((0, KC), (1, KC), (2, FC)))

            def load_expert(e, n):
                for i, (dst, name) in enumerate(((w_gate, "w_exp_gate"), (w_up, "w_exp_up"), (w_down, "w_exp_down"))):
                    sp.wait_ge(e_step, n * 4 + (1, 2, 4)[i])
                    sp.dma_start(dst, a[name][0, ds(e, 1), :, :].rearrange("o (k p) c -> p (o k) c", p=128)).then_inc(ew_loaded[i], 16)

            sp.wait_ge(wo_mm, 27)
            sp.wait_ge(mix_done, KC + 2)
            sp.wait_ge(tails_stored, 96)
            load_expert(0, 0)
            sp.wait_ge(pass_ready, 1)
            n_pass = sp.value_load(npass_i[0:1, 0:1], min_val=1, max_val=PASSES)
            with sp.Fori(1, n_pass * NE) as n:
                sp.wait_ge(comb_done, (n // NE) * (2 * NT) + 2 * NT + 1)
                sp.sem_inc(wait_stop, 1)
                load_expert(n % NE, n)
            sp.wait_ge(e_step, n_pass * (4 * NE) + 2)
            sp.sem_inc(wait_stop, 1)
            sp.dma_start(w_ple_sb, a["w_ple"][0].rearrange("(k p) c -> p k c", p=128)).then_inc(ple_in, 16)
            sp.dma_start(gfin, a["g_final"].partition_broadcast(128)).then_inc(gfin_in, 16)
            with sp.Fori(0, 4) as i:
                for s in range(2):
                    sp.wait_ge(comb_done, n_pass * (2 * NT) + 2 * s + 3)
                    sp.sem_inc(wait_stop, 1)
                    sp.wait_ge(ple_mm, 6 * i + 3 * s + 1)
                    sp.sem_inc(wait_stop, 1)
                    sp.dma_start(slab[s], cols(a["w_ple_gate"], i * 512 + s * SLAB)).then_inc(pslab[s], 16)
            for t in range(NT):
                sp.wait_ge(f_ok, t + 1)
                dst = y_p[0, t * 128:(t + 1) * 128, :] if t < 2 else y_s.rearrange("b s d -> (b s) d")
                sp.dma_start(dst, yfin[t]).then_inc(f_out[t], 16)

        @block.gpsimd
        def _(pool):
            pool.memset(slot[5][:, 0:384], 0.0).then_inc(consts_ready, 1)
            pool.memset(ident, 0.0).then_inc(consts_ready, 1)
            pool.memset(ones, 1.0).then_inc(consts_ready, 1)
            pool.memset(convmem[:, :, 0:HIST], 0.0).then_inc(consts_ready, 1)
            pool.wait_ge(consts_ready, 4)
            pool.affine_select(out=ident, in_=ident, compare_op=ALU.not_equal, fill=1.0, base=0,
                               pattern=[[-1, 128]], channel_multiplier=1).then_inc(consts_ready, 1)
            pool.affine_select(out=before, in_=ones, compare_op=ALU.is_gt, fill=0.0, base=0,
                               pattern=[[1, 128]], channel_multiplier=-1).then_inc(consts_ready, 1)
            pool.affine_select(out=causal[:, 0, :], in_=ones, compare_op=ALU.is_ge, fill=0.0, base=0,
                               pattern=[[1, 128]], channel_multiplier=-1).then_inc(consts_ready, 1)
            pool.affine_select(out=stream_of, in_=ones[:, 0:NSEQ], compare_op=ALU.is_ge, fill=0.0, base=0,
                               pattern=[[-SLEN, NSEQ]], channel_multiplier=1).then_inc(consts_ready, 1)
            pool.wait_ge(consts_ready, 8)
            pool.affine_select(out=stream_of, in_=stream_of, compare_op=ALU.is_ge, fill=0.0, base=SLEN - 1,
                               pattern=[[SLEN, NSEQ]], channel_multiplier=-1).then_inc(consts_ready, 1)
            pool.affine_select(out=v3(causal[:, 1, :], NSEQ), in_=v3(causal[:, 0, :], NSEQ), compare_op=ALU.is_ge,
                               fill=0.0, base=0, pattern=[[-SLEN, NSEQ], [0, SLEN]], channel_multiplier=1).then_inc(consts_ready, 1)
            pool.memset(rmask, 1.0).then_inc(consts_ready, 1)
            pool.wait_ge(consts_ready, 11)
            pool.memset(rmask[:, 0:SEQ].rearrange("p (c t) -> p c t", t=128)[:, :, 0:1], 0.0).then_inc(consts_ready, 1)
            pool.memset(rmask[:, SEQ:T].rearrange("p (c t) -> p c t", t=SLEN)[:, :, 0:1], 0.0).then_inc(consts_ready, 1)
            pool.iota(iota64, pattern=[[1, 64]], base=0, channel_multiplier=0, allow_small_or_imprecise_dtypes=True).then_inc(consts_ready, 1)
            assert CONSTS == 14
            pool.dma_start(hist_rows[:, 0:XBC], a["state_ssm_conv"][0].rearrange("b k c -> (b k) c")).then_inc(setup_in, 16)
            pool.dma_start(hist_rows[:, XBC:XBC + D], a["state_lru_conv"][0].rearrange("b k c -> (b k) c")).then_inc(setup_in, 16)
            pool.dma_start(sm[:, 0:128], a["state_lru"][0].rearrange("b (c p) -> (b c) p", p=128)).then_inc(setup_in, 16)
            pool.dma_start(dcol[:, 0:1], a["dt_bias"].rearrange("o h -> h o")).then_inc(setup_in, 16)
            pool.dma_start(dcol[:, 1:2], a["a_log"].rearrange("o h -> h o")).then_inc(setup_in, 16)
            for half in range(2):
                pool.dma_start(dskip[half * 64:(half + 1) * 64, :],
                               a["d_skip"][0].rearrange("(c h) -> h c", h=2)[half].partition_broadcast(64),
                               allow_slow_non_contiguous=True).then_inc(setup_in, 16)
            pool.wait_ge(dt_step, 3)
            pool.dma_start(acum_d, cumT).then_inc(cum_stored, 16)

            def load_h0(jj, parity):
                pool.dma_start(h0[parity], a["state_ssm"][0].rearrange("b (c h) p n -> (h p) c b n", h=2)[:, ds(jj, 1)].rearrange("q o b n -> q (o b) n")
                               ).then_inc(h0_loaded[parity], 16)
            pool.wait_ge(dt_tr, 1)
            for j in range(2):
                load_h0(j, j)

            def store_h(jj, parity):
                pool.wait_ge(hn_done, jj + 2)
                pool.dma_start(ssm_s[0].rearrange("b (c h) p n -> (h p) c b n", h=2)[:, ds(jj, 1)].rearrange("q o b n -> q (o b) n"),
                               h0[parity]).then_inc(hn_stored, 16)
                pool.wait_ge(hn_stored, jj * 16 + 16)

            with pool.Fori(0, KC // 2 - 1) as i:
                for j in range(2):
                    store_h(2 * i + j, j)
                    load_h0(2 * i + j + 2, j)
            for jj in (KC - 2, KC - 1):
                store_h(jj, jj % 2)
            pool.wait_ge(mix_mm, 4 * KC + 2)
            pool.wait_ge(tails_T, 11)
            for t in range(NT):
                src = a["x_prompt"][0, t * 128:(t + 1) * 128, :] if t < 2 else a["x_sample"].rearrange("b s d -> (b s) d")
                pool.dma_start(x_res[:, t, :], src).then_inc(x_again, 16)
            for t in range(NT):
                src = a["p_prompt"][0, 0, t * 128:(t + 1) * 128, :] if t < 2 else a["p_sample"][0].rearrange("b s d -> (b s) d")
                pool.dma_start(p_in[:, t, :], src).then_inc(p_loaded, 16)
            pool.dma_start(w_r[:, :, 0:EG], a["w_router_group"][0].rearrange("(k p) c -> p k c", p=128)).then_inc(router_in, 16)
            pool.dma_start(w_r[:, :, EG:36], a["w_router_expert"][0].rearrange("(k p) c -> p k c", p=128)).then_inc(router_in, 16)
            pool.dma_start(rbias[:, 0:EG], a["b_router_group"][0].partition_broadcast(128)).then_inc(router_in, 16)
            pool.dma_start(rbias[:, EG:36], a["b_router_expert"][0].partition_broadcast(128)).then_inc(router_in, 16)
            pool.iota(ie32, pattern=[[1, NE]], base=0, channel_multiplier=0, allow_small_or_imprecise_dtypes=True).then_inc(consts_ready, 1)
            pool.iota(ir32, pattern=[[-1, NE]], base=100, channel_multiplier=0, allow_small_or_imprecise_dtypes=True).then_inc(consts_ready, 1)
            pool.wait_ge(pass_ready, 1)
            n_pass = pool.value_load(npass_i[0:1, 0:1], min_val=1, max_val=PASSES)
            with pool.Fori(0, n_pass) as p:
                for h in range(2):
                    pool.wait_ge(yrow_out[h], p * (16 * NE) + 16 * NE + 1)
                pool.wait_ge(e_step, p * (4 * NE) + 4 * NE + 4)
                for n in range(2 * NT):
                    if n == 0:
                        pool.wait_ge(comb_done, p * (2 * NT) + 2 * NT + 1)
                        pool.sem_inc(wait_stop, 1)
                    pool.indirect_dma_start(out=cg[n], out_offset=None, in_=y_d[:, :],
                                            in_offset=bass.IndirectOffsetOnAxis(ap=ridx_col(n % 2, n // 2), axis=0)).then_inc(comb_in[n], 16)

        @block.scalar
        def _(act):
            A = nc.scalar.activation
            for started in (pst_stored, gu_act, *yrow_out):
                act.sem_inc(started, 1)
            act.sem_inc(proj_free, 2)
            act.sem_inc(silu_done, 2)
            act.sem_inc(dn_free, 2)
            act.sem_inc(l_sig, 2)

            n = 0
            def rows(src, at, count):
                done = 0
                while done < count:
                    r = at + done
                    m = min(count - done, 128 - r % 128)
                    act.dma_start(prow[r % 128:r % 128 + m, r // 128, :], src[done:done + m, :]).then_inc(params_in, 16)
                    done += m
                    nonlocal n
                    n += 1
            r16 = lambda ap: ap.rearrange("o (c p) -> (o c) p", p=128)
            act.wait_ge(consts_ready, 1)
            for name, at in (("g_mix", P_GMIX), ("g_ffn", P_GFFN), ("g_ple", P_GPLE), ("g_ssm", P_GSSM),
                             ("b_lru_a", P_BA), ("b_lru_x", P_BX), ("lru_lambda", P_LAM)):
                rows(r16(a[name]), at, 16)
            rows(r16(a["conv_m_b"]), P_CB, 24)
            rows(r16(a["conv_r_b"]), P_CB + 24, 16)
            rows(a["conv_m_w"].rearrange("o k (c p) -> (o k c) p", p=128), P_CW, 96)
            rows(a["conv_r_w"].rearrange("o k (c p) -> (o k c) p", p=128), P_CR, 64)
            assert n == PARAM_DMAS, n

            def square_tile(n, src):
                if n in (NT - 1, 3 * NT - 1):
                    act.wait_ge(n_tr, 4 * (n - 1))
                A(staging(n), src, ACT.Square, accum_out=sm[:, ss_c + n:ss_c + n + 1]).then_inc(n_sq, 1)
                act.wait_ge(n_ms, n + 1)
                A(sm[:, rt_c + n:rt_c + n + 1], sm[:, ms_c + n:ms_c + n + 1], ACT.Sqrt).then_inc(n_rt, 1)

            for t in range(NT):
                act.wait_ge(x_loaded[t], 16)
                square_tile(t, x_in[:, t, :])
            act.wait_ge(consts_ready, CONSTS)
            act.wait_ge(setup_in, 16 * 7)
            act.wait_ge(dt_step, 1)
            A(dA, dtmp2, ACT.Exp).then_inc(dt_act, 1)
            A(dcol[:, 2:3], dcol[:, 1:2], ACT.Exp).then_inc(dt_act, 1)
            act.wait_ge(dt_step, 2)
            A(ddT, cumT, ACT.Ln).then_inc(dt_act, 1)
            act.wait_ge(dt_step, 4)
            A(ddT, ddT, ACT.Exp).then_inc(dt_act, 1)
            A(dcol[:, 4:5], cumT[:, SEQ - 1:SEQ], ACT.Exp).then_inc(dt_act, 1)
            for b in range(2):
                act.wait_ge(hist_T, b + 1)
                A(convmem[:, 20 * b:20 * b + 20, HIST:27], v3(banks[6 + b][:, 0:480], 20), ACT.Copy).then_inc(hist_evac, 1)
            act.wait_ge(hist_T, 3)
            A(lru_h0, v3(banks[3][:, 0:128], NSEQ), ACT.Copy).then_inc(hist_evac, 1)
            act.wait_ge(dt_step, 6)
            A(sm[:, lam_s + 16:lam_s + 32], sm[:, lam_s:lam_s + 16], ACT.Exp).then_inc(dt_act, 1)
            act.wait_ge(dt_step, 7)
            A(sm[:, lam_s + 48:lam_s + 64], sm[:, lam_s + 32:lam_s + 48], ACT.Ln).then_inc(dt_act, 1)

            def to_padded(n, nconv, m):
                act.wait_ge(proj_done, n + 3)
                act.wait_ge(conv_done, nconv + 1)
                bank, r = banks[m % 2], raw[m % 2]
                A(r[:, HIST:S0], bank[:, 0:SEQ], ACT.Copy)
                A(pstreams(r)[:, :, HIST:SPAD], streams(bank[:, 0:T]), ACT.Copy).then_inc(proj_free, 1)

            with act.Fori(0, GROUPS) as g:
                conv_out = [BT, CT] + [xsT[:, j, :] for j in range(4)]

                def silu(m):
                    act.wait_ge(conv_done, 6 * g + m + 3)
                    c = acc[m % 2]
                    A(conv_out[m][:, 0:SEQ], c[:, 0:SEQ], ACT.Silu)
                    A(streams(conv_out[m]), pstreams(c)[:, :, 0:SLEN], ACT.Silu).then_inc(silu_done, 1)

                act.wait_ge(y_done, 4 * g + 1)
                for m in range(6):
                    to_padded(10 * g + m, 6 * g + m, m)
                    if m:
                        silu(m - 1)
                silu(5)
                for m in range(6, 10):
                    act.wait_ge(proj_done, 10 * g + m + 3)
                    A(Y[:, 4 * g + m - 6, :], banks[m % 2][:, 0:T], ACT.Silu).then_inc(proj_free, 1)
                    if m == 7:
                        act.wait_ge(seg_ready, g + 1)
                        A(decay, decay, ACT.Exp)
                        A(growth, growth, ACT.Exp).then_inc(exp_done, 1)
                act.wait_ge(hT0_done, g + 1)
                A(hT0, banks[7][:, :], ACT.Copy).then_inc(hT0_evac, 1)
                act.wait_ge(pst_done, g + 1)
                act.wait_ge(pst_stored, 16 * g + 1)
                A(pst, v3(banks[3][:, :], 4), ACT.Copy).then_inc(pst_evac, 1)
                act.wait_ge(pst_evac, g + 1)
                act.dma_start(ssm_p[0, 0].rearrange("(c h) p n -> (h p) c n", h=2)[:, ds(4 * g, 4), :], pst).then_inc(pst_stored, 16)
                for j in range(4):
                    act.wait_ge(h0_tr, 4 * g + j + 1)
                    act.wait_ge(y_mm, 4 * g + j + 1)
                    A(h0T[:, 0:4, :], v3(banks[2][:, :], 4), ACT.Copy)
                    A(h0T[:, 4:8, :], v3(banks[3][:, :], 4), ACT.Copy).then_inc(h0T_evac, 1)
                    act.wait_ge(y_done, 4 * g + j + 2)
                    A(ysq[j % 2], ytmp[j % 2], ACT.Square)
                    A(Y[:, 4 * g + j, :], ytmp[j % 2], ACT.Identity, scale=pcol[:, ds(4 * g + j + P_GSSM, 1)]).then_inc(y_act, 1)

            with act.Fori(0, GROUPS) as g:
                for m in range(4):
                    to_padded(8 * g + m + 40, 4 * g + m + 24, m)
                act.wait_ge(l_done, g + 1)
                for m in range(4, 8):
                    act.wait_ge(proj_done, 8 * g + m + 43)
                    A(gy[:, m - 4, :], banks[m % 2][:, 0:T], ACT.Gelu_apprx_tanh).then_inc(proj_free, 1)
                for m in range(4):
                    act.wait_ge(l_mm, 4 * g + m + 2)
                    b = 2 + 2 * (m % 2)
                    A(lr[:, m, :], banks[b][:, 0:T], ACT.Sigmoid, bias=pcol[:, ds(4 * g + m + P_BA, 1)])
                    A(li[:, m, :], banks[b + 1][:, 0:T], ACT.Sigmoid, bias=pcol[:, ds(4 * g + m + P_BX, 1)]).then_inc(l_sig, 1)
                act.wait_ge(l_la, g + 1)
                A(lr, la_, ACT.Exp)
                A(lt, la_, ACT.Tanh).then_inc(l_at, 1)
                act.wait_ge(l_w, g + 1)
                A(la_, lt, ACT.Sqrt).then_inc(l_s, 1)

            act.wait_ge(rs_ms, 1)
            A(rstdB, rstdB, ACT.Sqrt).then_inc(rs_rt, 1)

            act.wait_ge(l_done, GROUPS + 1)
            with act.Fori(0, 8) as i:
                for src, dst in ((0, sg_m), (2, sg_r)):
                    for cc in range(2):
                        act.wait_ge(mix_mm, 8 * i + 2 * src + cc + 3)
                        act.wait_ge(mix_done, 2 * i + cc + 1)
                        A(dst[cc], banks[2 * src + cc][:, 0:T], ACT.Sigmoid).then_inc(mix_sig, 1)

            for q in range(10):
                act.wait_ge(tails_T, q + 1)
                A(tail_rows[:, 512 * q:512 * q + 512], banks[4 + q % 2][0:27, :], ACT.Copy).then_inc(tails_evac, 1)
            act.wait_ge(tails_T, 11)
            A(sm[0:16, 0:128], banks[4][0:16, 0:128], ACT.Copy).then_inc(tails_evac, 1)
            A(lru_rows, banks[4][:, 128:256], ACT.Copy).then_inc(tails_evac, 1)
            act.wait_ge(tails_evac, 12)
            act.dma_start(sconv_p[0, 0], tail_rows[0:3, 0:XBC]).then_inc(tails_stored, 16)
            act.dma_start(lconv_p[0, 0], tail_rows[0:3, XBC:XBC + D]).then_inc(tails_stored, 16)
            act.dma_start(sconv_s[0].rearrange("b k c -> (b k) c"), tail_rows[3:27, 0:XBC]).then_inc(tails_stored, 16)
            act.dma_start(lconv_s[0].rearrange("b k c -> (b k) c"), tail_rows[3:27, XBC:XBC + D]).then_inc(tails_stored, 16)
            act.dma_start(lru_p[0, 0].rearrange("(c p) -> c p", p=128), sm[0:16, 0:128]).then_inc(tails_stored, 16)
            act.dma_start(lru_s[0].rearrange("b (c p) -> (b c) p", p=128), lru_rows).then_inc(tails_stored, 16)

            for t in range(NT):
                act.wait_ge(wo_done, 24 + 6)
                square_tile(NT + t, x_res[:, t, :])
            act.wait_ge(p_T, 1)
            A(pT[:, 0, :], banks[6][:, 0:T], ACT.Copy).then_inc(p_evac, 1)
            A(pT[:, 1, :], banks[7][:, 0:T], ACT.Copy).then_inc(p_evac, 1)
            act.wait_ge(r_lt, 1)
            A(ge, ge, ACT.Exp).then_inc(r_exp, 1)
            act.wait_ge(r_lt, 2)
            A(rcol[:, 8, :], rcol[:, 8, :], ACT.Exp).then_inc(r_exp, 1)

            act.wait_ge(pass_ready, 1)
            n_pass = act.value_load(npass_i[0:1, 0:1], min_val=1, max_val=PASSES)
            with act.Fori(0, n_pass) as p:
                act.wait_ge(comb_done, p * (2 * NT) + 2 * NT + 1)
                with act.Fori(0, PAIRS) as q:
                    for x in range(2):
                        E = p * NE + 2 * q + x
                        act.wait_ge(e_step, 4 * E + 4 + 1)
                        act.wait_ge(gu_done, E + 1)
                        A(hrow[x], banks[2 * x][:, 0:FF // 2], ACT.Silu).then_inc(gu_act, 1)
                        for j in range(2):
                            act.wait_ge(e_step, 4 * E + 4 + 3 + j)
                            if j == 0:
                                for h in range(2):
                                    act.wait_ge(yrow_out[h], 16 * E + 1)
                            A(yrow[:, j, :], banks[6 + j][:, :], ACT.Copy).then_inc(dn_free, 1)
                        act.wait_ge(dn_free, 2 * E + 4)
                        for h in range(2):
                            act.dma_start(y_d[ds((2 * q + x) * SLOTS, SLOTS), :].rearrange("s (j h c) -> h s j c", j=2, h=2)[h],
                                          yrow[h * SLOTS:(h + 1) * SLOTS, :, :]).then_inc(yrow_out[h], 16)

            for t in range(NT):
                act.wait_ge(comb_done, n_pass * (2 * NT) + 2 * t + 3)
                square_tile(2 * NT + t, x_res[:, t, :])
            with act.Fori(0, 4) as i:
                for n in range(6):
                    act.wait_ge(ple_mm, 6 * i + n + 4)
                    act.wait_ge(ple_done, 6 * i + n + 5)
                    A(gsig[n % 2], banks[n][:, 0:SLAB], ACT.Sigmoid).then_inc(ple_sig, 1)
            act.wait_ge(gfin_in, 16)
            for t in range(NT):
                act.wait_ge(ple_done, 18 + 6 + 4 + t)
                A(yfin[t], x_res[:, t, :], ACT.Square, accum_out=sm[:, t:t + 1]).then_inc(f_sq, 1)
                act.wait_ge(f_ms, t + 1)
                A(sm[:, 8 + t:9 + t], sm[:, 4 + t:5 + t], ACT.Sqrt).then_inc(f_rt, 1)
            for t in range(NT):
                act.wait_ge(f_out[t], 16)
            act.wait_ge(tails_stored, 96)
            act.wait_ge(pst_stored, 16 * GROUPS + 1)
            act.wait_ge(hn_stored, 16 * KC)

        @block.vector
        def _(dve):
            V = nc.vector
            link = Chain(dve, dch)
            TT, TS, STT = V.tensor_tensor, V.tensor_scalar, V.scalar_tensor_tensor
            for started in (y_done, hn_done, l_done, gu_done):
                dve.sem_inc(started, 1)
            dve.sem_inc(comb_done, 2 * NT + 1)
            dve.sem_inc(conv_done, 2)
            dve.sem_inc(n_evac, 4)
            dve.sem_inc(y_free, 1)
            dve.sem_inc(mix_done, 2)
            dve.sem_inc(wo_done, 6)
            dve.sem_inc(ple_done, 6)
            V.memset(ss_acc, 0.0)

            def norm_tile(n, src, gain, dst, t):
                dve.wait_ge(n_sq, n + 1)
                TS(sm[:, ms_c + n:ms_c + n + 1], sm[:, ss_c + n:ss_c + n + 1], 1.0 / D, EPS, ALU.mult, ALU.add).then_inc(n_ms, 1)
                dve.wait_ge(n_rt, n + 1)
                rstd = sm[:, rstd_c + n:rstd_c + n + 1]
                link(V.reciprocal(rstd, sm[:, rt_c + n:rt_c + n + 1]))
                TS(staging(n), src, rstd, None, ALU.mult).then_inc(n_scaled, 1)
                for b in range(4):
                    dve.wait_ge(n_tr, 4 * n + b + 1)
                    TT(dst[:, 4 * b:4 * b + 4, t * 128:(t + 1) * 128], v3(banks[b][:, :], 4),
                       spread(pcol[:, gain + 4 * b:gain + 4 * b + 4], 128), ALU.mult).then_inc(n_evac, 1)

            dve.wait_ge(ptr_done, 1)
            link(V.tensor_copy(pcol, banks[6][:, 0:384]))
            for t in range(NT):
                norm_tile(t, x_in[:, t, :], P_GMIX, xnT, t)

            dve.wait_ge(dt_done, 1)
            dve.wait_ge(setup_in, 16 * 7)
            dve.wait_ge(consts_ready, CONSTS)
            link(TS(dtmp, banks[4][0:HEADS, 0:T], dcol[:, 0:1], None, ALU.add))
            STT(dtmp2, dtmp, -1.0, dtmp, ALU.mult, ALU.min).then_inc(dt_step, 1)
            dve.wait_ge(dt_act, 2)
            TS(cumT, dA, 1.0, None, ALU.add).then_inc(dt_step, 1)
            dve.wait_ge(dt_act, 3)
            link(TS(cumT, cumT, 1.0, 1e-30, ALU.subtract, ALU.max))
            link(V.reciprocal(cumT, cumT))
            link(TT(dA, dA, cumT, ALU.mult))
            link(TT(ddT, ddT, dA, ALU.mult))
            link(STT(dtT, dtmp, 0.0, ddT, ALU.max, ALU.add))
            link(TS(dcol[:, 3:4], dcol[:, 2:3], -1.0, None, ALU.mult))
            link(TS(dA, dtT, dcol[:, 3:4], None, ALU.mult))
            V.tensor_tensor_scan(cumT, rmask, dA, 0.0, ALU.mult, ALU.add).then_inc(dt_step, 1)
            dve.wait_ge(dt_step, 3)
            for lo, hi, ln in ((0, SEQ, 128), (SEQ, T, SLEN)):
                seg = cumT[:, lo:hi].rearrange("p (c t) -> p c t", t=ln)
                last = TT(ddT[:, lo:hi].rearrange("p (c t) -> p c t", t=ln),
                          seg[:, :, ln - 1:ln].broadcast_to([HEADS, (hi - lo) // ln, ln]), seg, ALU.subtract)
            last.then_inc(dt_step, 1)
            dve.wait_ge(dt_act, 5)
            link(TT(ddT, ddT, dtT, ALU.mult))
            TS(ddfT, ddT[:, 0:128], dcol[:, 4:5], None, ALU.mult).then_inc(dt_step, 1)
            lam = pcol[:, P_LAM:P_LAM + 16]
            l0, l1, l2, l3 = (sm[:, lam_s + 16 * i:lam_s + 16 * i + 16] for i in range(4))
            STT(l0, lam, -1.0, lam, ALU.mult, ALU.min).then_inc(dt_step, 1)
            dve.wait_ge(dt_act, 6)
            TS(l2, l1, 1.0, None, ALU.add).then_inc(dt_step, 1)
            dve.wait_ge(dt_act, 7)
            link(TS(l2, l2, 1.0, 1e-30, ALU.subtract, ALU.max))
            link(V.reciprocal(l2, l2))
            link(TT(l1, l1, l2, ALU.mult))
            link(TT(l3, l3, l1, ALU.mult))
            link(TS(l0, lam, -1.0, 0.0, ALU.mult, ALU.max))
            link(TT(l0, l0, l3, ALU.add))
            link(TS(lam_c, l0, -8.0, None, ALU.mult))
            dve.wait_ge(dt_tr, 1)
            link(V.tensor_copy(tokcol, v3(banks[5][:, 0:320], 10)))

            def conv(nproj, nconv, m, c, tap, out):
                r, o = raw[m % 2], acc[m % 2]
                V.tensor_copy(r[:, 0:HIST], convmem[:, c, 0:HIST])
                link(V.tensor_copy(pstreams(r)[:, :, 0:HIST], convmem[:, c, HIST:27].rearrange("p (b t) -> p b t", t=HIST)))
                dve.wait_ge(proj_free, nproj + 3)
                if out is None:
                    dve.wait_ge(silu_done, nconv + 1)
                op = TS(o[:, 0:CONV], r[:, 0:CONV], tap(0), pcol[:, ds(c + P_CB, 1)], ALU.mult, ALU.add)
                V.tensor_copy(convmem[:, c, 0:HIST], r[:, SEQ:S0])
                V.tensor_copy(convmem[:, c, HIST:27].rearrange("p (b t) -> p b t", t=HIST), pstreams(r)[:, :, SLEN:SPAD])
                link(op)
                for k in range(1, TAPS - 1):
                    link(STT(o[:, 0:CONV], r[:, k:k + CONV], tap(k), o[:, 0:CONV], ALU.mult, ALU.add))
                k = TAPS - 1
                if out is None:
                    STT(o[:, 0:CONV], r[:, k:k + CONV], tap(k), o[:, 0:CONV], ALU.mult, ALU.add).then_inc(conv_done, 1)
                else:
                    STT(out[:, 0:SEQ], r[:, k:k + SEQ], tap(k), o[:, 0:SEQ], ALU.mult, ALU.add)
                    STT(streams(out), pstreams(r)[:, :, HIST:SPAD], tap(k), pstreams(o)[:, :, 0:SLEN], ALU.mult, ALU.add).then_inc(conv_done, 1)

            with dve.Fori(0, GROUPS) as g:
                link.loop(g, SSD_LINKS)
                dve.wait_ge(cum_loaded, 48 * g + 48)
                for t in range(NT):
                    d = decay[:, :, t * 128:(t + 1) * 128]
                    op = TT(d, d, spread(tokcol[:, C_CUM + t, ds(g * HPG, HPG)], 128), ALU.subtract)
                    op = link(op)
                TS(decay, decay, 0.0, None, ALU.min).then_inc(seg_ready, 1)
                for m in range(6):
                    c = (g + 16, g + 20, 4 * g, 4 * g + 1, 4 * g + 2, 4 * g + 3)[m]
                    conv(10 * g + m, 6 * g + m, m, c, lambda k: pcol[:, ds(c + (P_CW + 24 * k), 1)], None)
                dve.wait_ge(aux_done, 5 * g + 1)
                TT(cbm[:, 0:2, :], v3(banks[2][:, 0:256], 2), spread_mid(causal[:, 0, :], 2), ALU.mult)
                link(TT(cbm[:, 2, :], banks[2][:, 256:384], causal[:, 1, :], ALU.mult))
                dve.wait_ge(aux_done, 5 * g + 2)
                link(V.tensor_copy(Btok, v3(banks[3][:, 0:384], 3)))
                link(TT(Bseg, spread_mid(Btok[:, 2, :], NSEQ), spread(stream_of, NST), ALU.mult))
                for t in range(NT):
                    dve.wait_ge(aux_done, 5 * g + 3 + t)
                    bank = v3(banks[4 + t][:, :], HPG)
                    kinds = [(x_dt[:, t, :], C_DT + t), (x_dd[:, t, :], C_DD + t)] + [(x_ddf, C_DDF)] * (t == 0)
                    for dst, col in kinds:
                        last = TT(v3(dst, HPG), bank, spread(tokcol[:, col, ds(g * HPG, HPG)], HP), ALU.mult)
                    last.then_inc(aux_evac, 1)
                dve.wait_ge(exp_done, g + 1)
                for t in range(NT):
                    d = decay[:, :, t * 128:(t + 1) * 128]
                    last = TT(d, d, spread_mid(cbm[:, t, :], HPG), ALU.mult)
                last.then_inc(w_ready, 1)
                for j in range(4):
                    yt, gr = ytmp[j % 2], growth[:, j, :]
                    dve.wait_ge(y_mm, 4 * g + j + 2)
                    link(V.tensor_copy(dec, gr[:, SEQ + SLEN - 1:T:SLEN]))
                    link(TT(gr[:, 128:T], gr[:, 128:T], banks[4][:, 128:T], ALU.mult))
                    op = STT(yt, xsT[:, j, :], dskip[:, ds(4 * g + j, 1)], banks[5][:, 0:T], ALU.mult, ALU.add)
                    op.then_inc(y_free, 1)
                    dve.wait_ge(y_free, 4 * g + j + 2)
                    link(TT(yt[:, 128:T], yt[:, 128:T], gr[:, 128:T], ALU.add))
                    TT(yt, yt, Y[:, 4 * g + j, :], ALU.mult).then_inc(y_done, 1)
                    hb = h0[j % 2]
                    dve.wait_ge(st_mm, 4 * g + j + 1)
                    link(TT(hb, hb, spread(dec, NST), ALU.mult))
                    TT(hb[:, 0:4, :], hb[:, 0:4, :], v3(banks[6][:, :], 4), ALU.add)
                    TT(hb[:, 4:8, :], hb[:, 4:8, :], v3(banks[7][:, :], 4), ALU.add).then_inc(hn_done, 1)
                    dve.wait_ge(y_act, 4 * g + j + 1)
                    link(TT(ss_acc, ss_acc, ysq[j % 2], ALU.add))
                link.end(GROUPS, SSD_LINKS)

            dve.wait_ge(hn_stored, 16 * KC)
            dve.wait_ge(pst_stored, 16 * GROUPS + 1)
            with dve.Fori(0, GROUPS) as g:
                link.loop(g, LRU_LINKS)
                for m in range(4):
                    c = 4 * g + m + 24
                    conv(8 * g + m + 40, 4 * g + m + 24, m, c, lambda k: pcol[:, ds(4 * g + m + (P_CR + 16 * k), 1)], xl[:, m, :])
                dve.wait_ge(l_sig, 4 * g + 4 + 2)
                for m in range(4):
                    last = TS(la_[:, m, :], lr[:, m, :], lam_c[:, ds(4 * g + m, 1)], None, ALU.mult)
                last.then_inc(l_la, 1)
                link(TT(li, li, xl, ALU.mult))
                dve.wait_ge(l_at, g + 1)
                link(TS(la_, lt, -1.0, 1.0, ALU.mult, ALU.add))
                link(V.reciprocal(la_, la_))
                STT(lt, lt, -2.0, la_, ALU.mult, ALU.mult).then_inc(l_w, 1)
                dve.wait_ge(l_s, g + 1)
                link(TT(li, li, la_, ALU.mult))
                first = slice(SEQ, T, SLEN)
                h_in = v3(lt[:, 0, 0:32], 4)
                link(TT(h_in, lr[:, :, first], lru_h0[:, :, ds(4 * g, 4)].rearrange("p b m -> p m b"), ALU.mult))
                link(TT(li[:, :, first], li[:, :, first], h_in, ALU.add))
                link(V.memset(lr[:, :, first], 0.0))
                for m in range(4):
                    last = V.tensor_tensor_scan(la_[:, m, :], lr[:, m, :], li[:, m, :], 0.0, ALU.mult, ALU.add)
                link(last)
                V.tensor_copy(lru_end[:, 0, ds(4 * g, 4)], la_[:, :, SEQ - 1])
                V.tensor_copy(lru_end[:, 1:9, ds(4 * g, 4)].rearrange("p b m -> p m b"), la_[:, :, SEQ + SLEN - 1:T:SLEN])
                dve.wait_ge(proj_free, 8 * g + 8 + 40 + 2)
                TT(H[:, ds(4 * g, 4), :], la_, gy, ALU.mult).then_inc(l_done, 1)
                link.end(GROUPS, LRU_LINKS)

            dve.wait_ge(rs_mm, 1)
            TS(rstdB, banks[6][:, 0:T], 1.0 / D, EPS, ALU.mult, ALU.add).then_inc(rs_ms, 1)
            dve.wait_ge(rs_rt, 1)
            link(V.reciprocal(rstdB, rstdB))

            with dve.Fori(0, 8) as i:
                link.loop(i, 6)
                for cc in range(2):
                    dve.wait_ge(mix_mm, 8 * i + 2 + cc + 3)
                    link(TT(t_m[cc], rstdB, banks[2 + cc][:, 0:T], ALU.mult))
                    dve.wait_ge(mix_sig, 4 * i + cc + 1)
                    link(TT(t_m[cc], t_m[cc], sg_m[cc], ALU.mult))
                for cc in range(2):
                    dve.wait_ge(mix_mm, 8 * i + 6 + cc + 3)
                    dve.wait_ge(mix_sig, 4 * i + 2 + cc + 1)
                    link(TT(t_r[cc], sg_r[cc], banks[6 + cc][:, 0:T], ALU.mult))
                    TT(mixed[:, 2 * i + cc, :], t_m[cc], t_r[cc], ALU.add).then_inc(mix_done, 1)
                link.end(8, 6)
            dve.wait_ge(x_again, 16 * NT)
            with dve.Fori(0, 4) as i:
                for n in range(6):
                    dve.wait_ge(wo_mm, 6 * i + n + 4)
                    xr = x_res[:, n % 3, ds(i * 512 + (n // 3) * SLAB, SLAB)]
                    TT(xr, xr, banks[n][:, 0:SLAB], ALU.add).then_inc(wo_done, 1)
            dve.wait_ge(wo_done, 24 + 6)
            for t in range(NT):
                norm_tile(NT + t, x_res[:, t, :], P_GFFN, xn2T, t)

            dve.wait_ge(router_in, 64)
            dve.wait_ge(consts_ready, CONSTS + 2)
            dve.wait_ge(r_mm, 1)
            R = lambda c: rcol[:, c, :]
            link(TT(L, v3(banks[4][:, 0:NT * 36], NT), spread_mid(rbias, NT), ALU.add))
            gl, el = L[:, :, 0:EG], L[:, :, EG:36]
            link(V.tensor_reduce(R(0), gl, AX.X, ALU.max))
            TT(ge, gl, spread(R(0), EG), ALU.subtract).then_inc(r_lt, 1)
            dve.wait_ge(r_lt, 1)
            link(TT(goh, gl, spread(R(0), EG), ALU.is_equal))
            link(TT(goh, goh, spread_mid(ir32[:, 0:EG], NT), ALU.mult))
            link(V.tensor_reduce(R(3), goh, AX.X, ALU.max))
            link(TT(goh, goh, spread(R(3), EG), ALU.is_equal))
            dve.wait_ge(r_exp, 1)
            link(V.tensor_reduce(R(1), ge, AX.X, ALU.add))
            link(V.reciprocal(R(2), R(1)))
            link(TS(goh, goh, 1.0, BIG, ALU.subtract, ALU.mult))
            for t in range(NT):
                op = TT(v3(em[:, t, :], EG), v3(el[:, t, :], EG), spread(goh[:, t, :], EPG), ALU.add)
            link(op)
            link(V.tensor_reduce(R(4), em, AX.X, ALU.max))

            def first_of(oh, vals, top, cand):
                link(TT(oh, vals, spread(top, NE), ALU.is_equal))
                link(TT(oh, oh, spread_mid(ir32, NT), ALU.mult))
                link(V.tensor_reduce(cand, oh, AX.X, ALU.max))
                link(TT(oh, oh, spread(cand, NE), ALU.is_equal))

            first_of(oh1, em, R(4), R(5))
            link(STT(em2, oh1, -3.0 * BIG, em, ALU.mult, ALU.add))
            link(V.tensor_reduce(R(6), em2, AX.X, ALU.max))
            TT(R(8), R(6), R(4), ALU.subtract).then_inc(r_lt, 1)
            first_of(oh2, em2, R(6), R(7))
            TT(Msel, oh1, oh2, ALU.add).then_inc(r_step, 1)
            dve.wait_ge(r_exp, 2)
            link(TS(R(9), R(8), 1.0, None, ALU.add))
            link(V.reciprocal(R(9), R(9)))
            link(TT(R(10), R(2), R(9), ALU.mult))
            link(V.tensor_copy(eweight[:, 0, :], R(10)))
            link(TT(eweight[:, 1, :], R(10), R(8), ALU.mult))
            dve.wait_ge(rank_mm, 1)
            link(V.tensor_copy(rankm, v3(banks[5][:, 0:NT * NE], NT)))
            link(V.tensor_reduce(rrow[:, 0:1], banks[6][:, 0:NE], AX.X, ALU.max))
            link(TS(rrow[:, 8:8 + PASSES], iota64[:, 0:PASSES], float(SLOTS), None, ALU.mult))
            link(TT(rrow[:, 8:8 + PASSES], rrow[:, 0:1].broadcast_to([128, PASSES]), rrow[:, 8:8 + PASSES], ALU.is_gt))
            link(V.tensor_reduce(rrow[:, 1:2], rrow[:, 8:8 + PASSES], AX.X, ALU.add))
            for k, oh in enumerate((oh1, oh2)):
                link(TT(c1, oh, spread_mid(ie32, NT), ALU.mult))
                link(V.tensor_reduce(R(12 + 2 * k), c1, AX.X, ALU.add))
                link(TT(c1, oh, rankm, ALU.mult))
                link(V.tensor_reduce(R(13 + 2 * k), c1, AX.X, ALU.add))
                link(TS(R(12 + 2 * k), R(12 + 2 * k), float(SLOTS), None, ALU.mult))
            link(STT(rankm, Msel, 1000.0, rankm, ALU.mult, ALU.add))
            link(TS(rankm, rankm, 1000.0, None, ALU.subtract))
            V.tensor_copy(npass_i[:, 0:1], rrow[:, 1:2]).then_inc(pass_ready, 1)
            dve.wait_ge(pass_ready, 1)

            n_pass = dve.value_load(npass_i[0:1, 0:1], min_val=1, max_val=PASSES)
            dve.sem_inc(xe_evac, 2)
            mlink = Chain(dve, mch)
            with dve.Fori(0, n_pass) as p:
                mlink.loop(p, 13)
                for k in range(2):
                    expert, rank = R(12 + 2 * k), R(13 + 2 * k)
                    mlink(TS(R(17), rank, float(SLOTS), None, ALU.is_lt))
                    mlink(STT(R(17), rank, 0.0, R(17), ALU.is_ge, ALU.mult))
                    mlink(TT(R(18), expert, rank, ALU.add))
                    mlink(TT(R(18), R(18), R(17), ALU.mult))
                    V.tensor_copy(ridx[:, k * NT:(k + 1) * NT], R(18))
                    mlink(TT(pweight[:, k, :], eweight[:, k, :], R(17), ALU.mult))
                    mlink(TS(rank, rank, float(SLOTS), None, ALU.subtract))

                def next_pick(q):
                    for t in range(NT):
                        last = TT(pick[:, t, :].rearrange("p (e s) -> p e s", s=SLOTS),
                                  spread(rankm[:, t, ds(q * 2, 2)] if not isinstance(q, int) else rankm[:, t, 2 * q:2 * q + 2], SLOTS),
                                  spread_mid(iota64, 2), ALU.is_equal)
                    last.then_inc(pick_ready, 1)

                def next_tokens(n):
                    for b in range(4):
                        dve.wait_ge(xe_tr, n * 4 + b + 2)
                        TT(xe[:, 4 * b:4 * b + 4, :], v3(banks[4 + b % 2][:, :], 4),
                           spread(pcol[:, P_GFFN + 4 * b:P_GFFN + 4 * b + 4], 128), ALU.mult).then_inc(xe_evac, 1)

                next_pick(0)
                next_tokens(p * (PAIRS + 1))
                with dve.Fori(0, PAIRS) as q:
                    next_pick((q + 1) % PAIRS)
                    for x in range(2):
                        E = p * NE + 2 * q + x
                        dve.wait_ge(e_step, 4 * E + 4 + 2)
                        dve.wait_ge(gu_act, E + 2)
                        TT(hrow[x], hrow[x], banks[2 * x + 1][:, 0:FF // 2], ALU.mult).then_inc(h_mul, 1)
                        if x == 1:
                            next_tokens(p * (PAIRS + 1) + q + 1)
                        dve.wait_ge(h_tr, E + 1)
                        dve.wait_ge(e_step, 4 * E + 4)
                        V.tensor_copy(hid[x], v3(banks[2 * x + 1][:, FF // 2:FF], FC)).then_inc(gu_done, 1)
                dve.wait_ge(pick_ready, p * (PAIRS + 1) + PAIRS + 1)
                mlink(TS(rankm, rankm, float(SLOTS), None, ALU.subtract))
                for n in range(2 * NT):
                    k, t = n % 2, n // 2
                    dve.wait_ge(comb_in[n], p * 16 + 16)
                    STT(x_res[:, t, :], cg[n], pweight[:, k, t:t + 1], x_res[:, t, :], ALU.mult, ALU.add).then_inc(comb_done, 1)
                    dve.wait_ge(comb_done, p * (2 * NT) + 2 * NT + n + 2)
                mlink.end(1, 13)

            for t in range(NT):
                norm_tile(2 * NT + t, x_res[:, t, :], P_GPLE, xn2T, t)
            with dve.Fori(0, 4) as i:
                for n in range(6):
                    dve.wait_ge(ple_sig, 6 * i + n + 1)
                    xr = x_res[:, n % 3, ds(i * 512 + (n // 3) * SLAB, SLAB)]
                    TT(gsig[n % 2], gsig[n % 2], banks[n][:, SLAB:2 * SLAB], ALU.mult).then_inc(ple_step, 1)
                    dve.wait_ge(ple_step, 6 * i + n + 1)
                    TT(xr, xr, gsig[n % 2], ALU.add).then_inc(ple_done, 1)
            for t in range(NT):
                dve.wait_ge(f_sq, t + 1)
                TS(sm[:, 4 + t:5 + t], sm[:, t:t + 1], 1.0 / D, EPS, ALU.mult, ALU.add).then_inc(f_ms, 1)
                dve.wait_ge(f_rt, t + 1)
                V.reciprocal(sm[:, 12 + t:13 + t], sm[:, 8 + t:9 + t]).then_inc(f_rc, 1)
                dve.wait_ge(f_rc, t + 1)
                STT(yfin[t], x_res[:, t, :], sm[:, 12 + t:13 + t], gfin, ALU.mult, ALU.mult).then_inc(f_ok, 1)

        @block.tensor
        def _(pe):
            mm, tr = nc.tensor.matmul, nc.tensor.transpose
            pe.sem_inc(proj_done, 2)
            for started in (y_mm, l_mm, xe_tr):
                pe.sem_inc(started, 1)
            pe.sem_inc(mix_mm, 2)
            pe.sem_inc(wo_mm, 3)
            pe.sem_inc(ple_mm, 3)
            pe.sem_inc(e_step, 4)
            pe.wait_ge(consts_ready, CONSTS)
            pe.wait_ge(params_in, 16 * PARAM_DMAS)
            for b in range(3):
                last = tr(banks[6][:, 128 * b:128 * b + 128], prow[:, b, :], ident)
            last.then_inc(ptr_done, 1)

            def norm_T(n):
                pe.wait_ge(n_scaled, n + 1)
                for b in range(4):
                    pe.wait_ge(n_evac, 4 * n + b + 1)
                    for q in range(4):
                        last = tr(banks[b][:, 128 * q:128 * q + 128], staging(n)[:, (4 * b + q) * 128:(4 * b + q + 1) * 128], ident)
                    last.then_inc(n_tr, 1)

            for t in range(NT):
                norm_T(t)
            pe.wait_ge(n_evac, 12 + 4)
            pe.wait_ge(dt_loaded, 16)
            for k in range(KC):
                last = mm(banks[4][0:HEADS, 0:T], w_dt[:, k, :], xnT[:, k, :], start=(k == 0), stop=(k == KC - 1))
            last.then_inc(dt_done, 1)
            pe.wait_ge(setup_in, 16 * 7)
            for b in range(2):
                for c in range(20):
                    last = tr(banks[6 + b][:, 24 * c:24 * c + 24], hist_rows[:, (20 * b + c) * 128:(20 * b + c + 1) * 128], ident[0:24, 0:24])
                last.then_inc(hist_T, 1)
            tr(banks[3][:, 0:128], sm[:, 0:128], ident).then_inc(hist_T, 1)

            def dt_columns():
                pe.wait_ge(dt_step, 5)
                for n, (src, t) in enumerate([(dtT, 0), (dtT, 1), (dtT, 2), (cumT, 0), (cumT, 1), (cumT, 2),
                                              (ddT, 0), (ddT, 1), (ddT, 2), (ddfT, 0)]):
                    last = tr(banks[5][:, 32 * n:32 * n + 32], src[:, t * 128:(t + 1) * 128], ident[0:32, 0:32])
                last.then_inc(dt_tr, 1)
            dt_columns()
            pe.wait_ge(hist_evac, 3)

            with pe.Fori(0, GROUPS) as g:
                def group_slab(m, w):
                    for c in range(2):
                        pe.wait_ge(proj_free, 10 * g + m + c + 1)
                        for k in range(KC):
                            last = mm(banks[(m + c) % 2][:, 0:T], w[:, k, c * 128:(c + 1) * 128], xnT[:, k, :],
                                      start=(k == 0), stop=(k == KC - 1))
                        last.then_inc(proj_done, 1)
                pe.wait_ge(side_loaded, 32 * g + 32)
                group_slab(0, slab[2])
                pe.wait_ge(slab_loaded[0], 32 * g + 16)
                group_slab(2, slab[0])
                pe.wait_ge(slab_loaded[1], 32 * g + 16)
                group_slab(4, slab[1])
                pe.wait_ge(slab_loaded[0], 32 * g + 32)
                group_slab(6, slab[0])
                pe.wait_ge(silu_done, 6 * g + 6 + 2)
                pe.wait_ge(y_free, 4 * g + 1)
                pe.wait_ge(hn_done, 4 * g + 1)
                for t in range(NT):
                    last = mm(banks[2][:, t * 128:(t + 1) * 128], BT[:, t * 128:(t + 1) * 128], CT[:, t * 128:(t + 1) * 128],
                              start=True, stop=True)
                last.then_inc(aux_done, 1)
                for t in range(NT):
                    last = tr(banks[3][:, t * 128:(t + 1) * 128], BT[:, t * 128:(t + 1) * 128], ident)
                last.then_inc(aux_done, 1)
                for t in range(NT):
                    for j in range(4):
                        last = tr(banks[4 + t][:, j * 128:(j + 1) * 128], xsT[:, j, t * 128:(t + 1) * 128], ident)
                    last.then_inc(aux_done, 1)
                pe.wait_ge(slab_loaded[1], 32 * g + 32)
                group_slab(8, slab[1])
                pe.wait_ge(aux_evac, 3 * g + 3)
                mm(banks[7][:, :], Btok[:, 0, :], x_dd[:, 0, :], start=True, stop=True).then_inc(hT0_done, 1)
                for j in range(4):
                    mm(banks[3][:, j * 128:(j + 1) * 128], x_ddf[:, j * 128:(j + 1) * 128], Btok[:, 0, :], start=True, stop=False)
                    last = mm(banks[3][:, j * 128:(j + 1) * 128], x_dd[:, 1, j * 128:(j + 1) * 128], Btok[:, 1, :], start=False, stop=True)
                last.then_inc(pst_done, 1)
                pe.wait_ge(w_ready, g + 1)
                pe.wait_ge(hT0_evac, g + 1)
                pe.wait_ge(pst_evac, g + 1)
                for j in range(4):
                    pe.wait_ge(h0_loaded[j % 2], 32 * g + 16 * (j // 2 + 1))
                    for b in range(NSEQ):
                        last = tr(banks[2 + b // 4][:, (b % 4) * 128:(b % 4 + 1) * 128], h0[j % 2][:, b, :], ident)
                    last.then_inc(h0_tr, 1)
                    pe.wait_ge(y_free, 4 * g + j + 1)
                    for t in range(NT):
                        for h in range(2):
                            mm(banks[5][h * 64:h * 64 + 64, t * 128:(t + 1) * 128],
                               x_dt[:, t, j * 128 + h * 64:j * 128 + h * 64 + 64],
                               decay[:, 2 * j + h, t * 128:(t + 1) * 128], start=True, stop=True)
                    mm(banks[4][:, 128:256], hT0[:, j * 128:(j + 1) * 128], CT[:, 128:256], start=True, stop=True)
                    pe.wait_ge(h0T_evac, 4 * g + j + 1)
                    for b in range(NSEQ):
                        s = slice(SEQ + b * SLEN, SEQ + (b + 1) * SLEN)
                        last = mm(banks[4][:, s], h0T[:, b, :], CT[:, s], start=True, stop=True)
                    last.then_inc(y_mm, 1)
                    pe.wait_ge(hn_done, 4 * g + j + 1)
                    for half in range(2):
                        last = mm(banks[6 + half][:, :], x_dd[:, 2, j * 128:(j + 1) * 128], Bseg[:, 4 * half:4 * half + 4, :],
                                  start=True, stop=True)
                    last.then_inc(st_mm, 1)

            with pe.Fori(0, GROUPS) as g:
                for s in range(4):
                    pe.wait_ge(slab_loaded[s % 2], 32 * g + (s // 2) * 16 + 128 + 16)
                    for c in range(2):
                        m = 2 * s + c
                        pe.wait_ge(proj_free, 8 * g + m + 41)
                        for k in range(KC):
                            last = mm(banks[m % 2][:, 0:T], slab[s % 2][:, k, c * 128:(c + 1) * 128], xnT[:, k, :],
                                      start=(k == 0), stop=(k == KC - 1))
                        last.then_inc(proj_done, 1)
                pe.wait_ge(side_loaded, 32 * g + 128 + 32)
                pe.wait_ge(conv_done, 4 * g + 24 + 4 + 2)
                pe.wait_ge(h0T_evac, KC)
                pe.wait_ge(hn_done, KC + 1)
                for m in range(4):
                    pe.wait_ge(l_sig, 4 * g + m + 1)
                    b = 2 + 2 * (m % 2)
                    mm(banks[b][:, 0:T], lw[:, m, :], xl[:, m, :], start=True, stop=True)
                    mm(banks[b + 1][:, 0:T], lw[:, 4 + m, :], xl[:, m, :], start=True, stop=True).then_inc(l_mm, 1)

            mm(banks[6][:, 0:T], ones, ss_acc, start=True, stop=True).then_inc(rs_mm, 1)
            pe.wait_ge(proj_free, 72 + 2)

            with pe.Fori(0, 8) as i:
                for s, rhs in enumerate((xnT, Y, xnT, H)):
                    if s == 1:
                        pe.wait_ge(l_sig, KC + 2)
                        pe.wait_ge(y_act, KC)
                    if s == 3:
                        pe.wait_ge(l_done, GROUPS + 1)
                        pe.wait_ge(rs_ms, 1)
                    pe.wait_ge(slab_loaded[s % 2], 32 * i + (s // 2) * 16 + 256 + 16)
                    for cc in range(2):
                        pe.wait_ge(mix_done, 2 * i + cc + 1)
                        for k in range(KC):
                            last = mm(banks[2 * s + cc][:, 0:T], slab[s % 2][:, k, cc * 128:(cc + 1) * 128], rhs[:, k, :],
                                      start=(k == 0), stop=(k == KC - 1))
                        last.then_inc(mix_mm, 1)
            pe.wait_ge(mix_sig, 32)
            for q in range(10):
                if q >= 2:
                    pe.wait_ge(tails_evac, q - 1)
                for r in range(4):
                    last = tr(banks[4 + q % 2][0:27, r * 128:(r + 1) * 128], convmem[:, 4 * q + r, :], ident)
                last.then_inc(tails_T, 1)
            pe.wait_ge(tails_evac, 9)
            tr(banks[4][0:16, 0:128], lru_end[:, 0, :], ident)
            tr(banks[4][:, 128:256], lru_end[:, 1:9, :], ident).then_inc(tails_T, 1)
            pe.wait_ge(mix_done, KC + 2)
            pe.wait_ge(tails_evac, 12)
            with pe.Fori(0, 4) as i:
                for s in range(2):
                    pe.wait_ge(slab_loaded[s], 16 * i + 512 + 16)
                    for t in range(NT):
                        pe.wait_ge(wo_done, 6 * i + 3 * s + t + 1)
                        for k in range(KC):
                            last = mm(banks[3 * s + t][:, 0:SLAB], mixed[:, k, t * 128:(t + 1) * 128], slab[s][:, k, :],
                                      start=(k == 0), stop=(k == KC - 1))
                        last.then_inc(wo_mm, 1)
            for t in range(NT):
                norm_T(NT + t)
            pe.wait_ge(p_loaded, 16 * NT)
            for h in range(2):
                for t in range(NT):
                    last = tr(banks[6 + h][:, t * 128:(t + 1) * 128], p_in[:, t, h * 128:(h + 1) * 128], ident)
            last.then_inc(p_T, 1)
            pe.wait_ge(n_evac, 24 + 4)
            pe.wait_ge(router_in, 64)
            for t in range(NT):
                for k in range(KC):
                    last = mm(banks[4][:, t * 36:t * 36 + 36], xn2T[:, k, t * 128:(t + 1) * 128], w_r[:, k, :],
                              start=(k == 0), stop=(k == KC - 1))
            last.then_inc(r_mm, 1)
            pe.wait_ge(r_step, 1)
            pe.wait_ge(p_evac, 2)
            for t in range(NT):
                for s in range(t + 1):
                    mm(banks[5][:, t * NE:(t + 1) * NE], before if s == t else ones, Msel[:, s, :], start=(s == 0), stop=(s == t))
            for t in range(NT):
                last = mm(banks[6][:, 0:NE], ones, Msel[:, t, :], start=(t == 0), stop=(t == NT - 1))
            last.then_inc(rank_mm, 1)

            pe.wait_ge(pass_ready, 1)
            n_pass = pe.value_load(npass_i[0:1, 0:1], min_val=1, max_val=PASSES)
            with pe.Fori(0, n_pass) as p:
                def pick_tokens(n):
                    pe.wait_ge(pick_ready, n + 1)
                    for b in range(4):
                        pe.wait_ge(xe_evac, n * 4 + b + 1)
                        for q4 in range(4):
                            for t in range(NT):
                                last = mm(banks[4 + b % 2][:, q4 * 128:(q4 + 1) * 128], xtok[t][:, (4 * b + q4) * 128:(4 * b + q4 + 1) * 128],
                                          pick[:, t, :], start=(t == 0), stop=(t == NT - 1))
                        last.then_inc(xe_tr, 1)

                pick_tokens(p * (PAIRS + 1))
                with pe.Fori(0, PAIRS) as q:
                    for x in range(2):
                        E = p * NE + 2 * q + x
                        pe.wait_ge(xe_evac, (p * (PAIRS + 1) + q) * 4 + 4 + 2)
                        pe.wait_ge(gu_done, E + 1)
                        for i, w in enumerate((v3(arena[:, 0:2 * SLABF], KC), v3(arena[:, 2 * SLABF:4 * SLABF], KC))):
                            pe.wait_ge(ew_loaded[i], 16 * E + 16)
                            for k in range(KC):
                                for h in range(2):
                                    last = mm(banks[2 * x + i][h * SLOTS:(h + 1) * SLOTS, 0:FF // 2], xe[:, k, x * SLOTS:(x + 1) * SLOTS],
                                              w[:, k, h * (FF // 2):(h + 1) * (FF // 2)], start=(k == 0), stop=(k == KC - 1))
                            last.then_inc(e_step, 1)
                        if x == 1:
                            pick_tokens(p * (PAIRS + 1) + q + 1)
                        pe.wait_ge(h_mul, E + 1)
                        for c in range(2):
                            last = tr(banks[2 * x + 1][:, FF // 2 + c * 128:FF // 2 + (c + 1) * 128], hrow[x][:, c * 128:(c + 1) * 128], ident)
                        last.then_inc(h_tr, 1)
                        pe.wait_ge(gu_done, E + 2)
                        pe.wait_ge(ew_loaded[2], 16 * E + 16)
                        wd = v3(arena[:, 4 * SLABF:6 * SLABF], FC)
                        for j in range(2):
                            pe.wait_ge(dn_free, 2 * E + j + 1)
                            for n in range(FC):
                                f = (n % 2) * 2 + n // 2
                                for h in range(2):
                                    last = mm(banks[6 + j][h * SLOTS:(h + 1) * SLOTS, :], hid[x][:, n, :],
                                              wd[:, f, (2 * j + h) * 512:(2 * j + h + 1) * 512], start=(n == 0), stop=(n == FC - 1))
                            last.then_inc(e_step, 1)

            for t in range(NT):
                norm_T(2 * NT + t)
            pe.wait_ge(n_evac, 36 + 4)
            pe.wait_ge(ple_in, 16)
            with pe.Fori(0, 4) as i:
                for s in range(2):
                    pe.wait_ge(pslab[s], 16 * i + 16)
                    for t in range(NT):
                        pe.wait_ge(ple_done, 6 * i + 3 * s + t + 1)
                        bank = banks[3 * s + t]
                        for k in range(KC):
                            mm(bank[:, 0:SLAB], xn2T[:, k, t * 128:(t + 1) * 128], slab[s][:, k, :], start=(k == 0), stop=(k == KC - 1))
                        for k in range(2):
                            last = mm(bank[:, SLAB:2 * SLAB], pT[:, k, t * 128:(t + 1) * 128], w_ple_sb[:, k, ds(i * 512 + s * SLAB, SLAB)],
                                      start=(k == 0), stop=(k == 1))
                        last.then_inc(ple_mm, 1)


_INS = ['x_prompt', 'x_sample', 'state_ssm', 'state_ssm_conv', 'state_lru', 'state_lru_conv', 'p_prompt', 'p_sample',
        'g_mix', 'w_in', 'conv_m_w', 'conv_m_b', 'dt_bias', 'a_log', 'd_skip', 'g_ssm', 'w_out_m',
        'conv_r_w', 'conv_r_b', 'w_lru_a', 'b_lru_a', 'w_lru_x', 'b_lru_x', 'lru_lambda', 'w_out_r', 'w_o',
        'g_ffn', 'w_router_group', 'b_router_group', 'w_router_expert', 'b_router_expert',
        'w_exp_gate', 'w_exp_up', 'w_exp_down', 'g_ple', 'w_ple_gate', 'w_ple', 'g_final']
_OUTS = [(1, SEQ, D), (NSEQ, SLEN, D),
         (1, 1, HEADS, HP, NST), (1, 1, HIST, XBC), (1, 1, D), (1, 1, HIST, D),
         (1, NSEQ, HEADS, HP, NST), (1, NSEQ, HIST, XBC), (1, NSEQ, D), (1, NSEQ, HIST, D)]


def kernel(**inputs):
    import numpy as _np
    import concourse.bacc as _bacc
    from concourse import mybir as _mybir
    from concourse.bass_utils import run_bass_kernel_spmd as _run

    nc = _bacc.Bacc("TRN2", target_bir_lowering=False, num_devices=1)
    arrays, ins = {}, {}
    f32 = _mybir.dt.float32
    for name in _INS:
        x = _np.ascontiguousarray(inputs[name])
        arrays[f"in_{name}_dram"] = x
        ins[name] = nc.dram_tensor(f"in_{name}_dram", x.shape, _mybir.dt.from_np(x.dtype), kind="ExternalInput").ap()
    outs = [nc.dram_tensor(f"out_{i}_dram", s, f32, kind="ExternalOutput").ap() for i, s in enumerate(_OUTS)]
    scratch = [nc.dram_tensor(n, s, f32).ap() for n, s in
               (("cumulated_decays", (HEADS, T)), ("expert_rows", (NE * SLOTS, D)))]
    hybrid_stream_step(nc, ins, outs, scratch)
    r = _run(nc, [arrays], core_ids=[0])
    return tuple(r.results[0][f"out_{i}_dram"] for i in range(len(_OUTS)))
```
